# Optimizing a Trainium2 kernel written in Bass

```python
import math
import jax
import jax.numpy as jnp
from jax import lax
import numpy as np

D_MODEL = 1024
BATCH = 1
SEQ = 1024
DEPTH = 2

GRID_W = 64
CTX_LEN = 256
HEAD_DIM = 64
ROPE_THETA = 10000.0
ROPE_PAIRS_PER_AXIS = HEAD_DIM // 4
QBLOCK = 128
WINDOW = 128
A_HEADS = 8
A_KV_HEADS = 2
B_HEADS = 4
B_V_DIM = 2 * HEAD_DIM
C_HEADS = 8
C_KV_HEADS = 2
N_BRANCHES = 3
A_WIDTH = A_HEADS * HEAD_DIM
B_WIDTH = B_HEADS * B_V_DIM
C_WIDTH = C_HEADS * HEAD_DIM
Q_SIZES = (A_HEADS * HEAD_DIM, B_HEADS * 2 * HEAD_DIM, C_HEADS * HEAD_DIM, N_BRANCHES * D_MODEL)
KV_SIZES = (A_KV_HEADS * HEAD_DIM, A_KV_HEADS * HEAD_DIM, B_HEADS * 2 * HEAD_DIM, B_HEADS * B_V_DIM,
            C_KV_HEADS * HEAD_DIM, C_KV_HEADS * HEAD_DIM)
Q_COLS = sum(Q_SIZES)
IN_COLS = Q_COLS + sum(KV_SIZES)
N_GROUPS = 4
EXPERTS_PER_GROUP = 8
N_EXPERTS = N_GROUPS * EXPERTS_PER_GROUP
TOP_K = 2
EXPERT_HIDDEN = D_MODEL // 2
N_MOD = 6
EPS = 1e-6
NEG_INF = -1e30

kernel_name = "hybrid_diffusion_backbone_ctx_prefix"

def rms_norm(x, gain=None):
    xf = x.astype(jnp.float32)
    y = xf * lax.rsqrt(jnp.mean(xf * xf, axis=-1, keepdims=True) + EPS)
    if gain is not None:
        y = y * gain.astype(jnp.float32)
    return y.astype(x.dtype)

def modulate(x, shift, scale):
    return x * (1 + scale) + shift

def split_cols(t, sizes):
    return jnp.split(t, np.cumsum(sizes)[:-1].tolist(), axis=-1)

def axial_rope_tables(n_tokens):
    rows = n_tokens // GRID_W
    row = jnp.repeat(jnp.arange(rows, dtype=jnp.float32), GRID_W)
    col = jnp.tile(jnp.arange(GRID_W, dtype=jnp.float32), rows)
    freqs = ROPE_THETA ** (-jnp.arange(ROPE_PAIRS_PER_AXIS, dtype=jnp.float32) / ROPE_PAIRS_PER_AXIS)
    ang = jnp.concatenate([row[:, None] * freqs, col[:, None] * freqs], axis=-1)
    return jnp.cos(ang), jnp.sin(ang)

def apply_rope(x, rope):
    cos, sin = rope
    shape = (cos.shape[0],) + (1,) * (x.ndim - 3) + (cos.shape[1],)
    cos, sin = cos.reshape(shape), sin.reshape(shape)
    half = HEAD_DIM // 2
    xf = x.astype(jnp.float32)
    x1, x2 = xf[..., :half], xf[..., half:]
    return jnp.concatenate([x1 * cos - x2 * sin, x1 * sin + x2 * cos], axis=-1).astype(x.dtype)

def split_queries(qg, P, rope):
    aq, bq, cq, gates = split_cols(qg, Q_SIZES)
    n, t = qg.shape[:2]
    aq = rms_norm(aq.reshape(n, t, A_HEADS, HEAD_DIM), P["a_qnorm"])
    bq = rms_norm(bq.reshape(n, t, B_HEADS, 2, HEAD_DIM), P["b_qnorm"])
    cq = rms_norm(cq.reshape(n, t, C_HEADS, HEAD_DIM), P["c_qnorm"])
    if rope is not None:
        aq, bq, cq = apply_rope(aq, rope), apply_rope(bq, rope), apply_rope(cq, rope)
    aq = aq.reshape(n, t, A_KV_HEADS, A_HEADS // A_KV_HEADS, HEAD_DIM)
    cq = cq.reshape(n, t, C_KV_HEADS, C_HEADS // C_KV_HEADS, HEAD_DIM)
    return aq, bq, cq, gates

def split_keys_values(kv, P, rope):
    ak, av, bk, bv, ck, cv = split_cols(kv, KV_SIZES)
    n, s = kv.shape[:2]
    ak = rms_norm(ak.reshape(n, s, A_KV_HEADS, HEAD_DIM), P["a_knorm"])
    bk = rms_norm(bk.reshape(n, s, B_HEADS, 2, HEAD_DIM), P["b_knorm"])
    ck = rms_norm(ck.reshape(n, s, C_KV_HEADS, HEAD_DIM), P["c_knorm"])
    if rope is not None:
        ak, bk, ck = apply_rope(ak, rope), apply_rope(bk, rope), apply_rope(ck, rope)
    av = av.reshape(n, s, A_KV_HEADS, HEAD_DIM)
    bv = bv.reshape(n, s, B_HEADS, B_V_DIM)
    cv = cv.reshape(n, s, C_KV_HEADS, HEAD_DIM)
    return ak, av, bk, bv, ck, cv

def gqa_attend(q, k, v, mask=None, sink=None):
    s = jnp.einsum("btkgd,bskd->bkgts", q, k).astype(jnp.float32) * (q.shape[-1] ** -0.5)
    if mask is not None:
        s = jnp.where(mask, s, NEG_INF)
    if sink is not None:
        snk = jnp.broadcast_to(sink.astype(jnp.float32).reshape(1, k.shape[2], -1, 1, 1), s.shape[:-1] + (1,))
        p = jax.nn.softmax(jnp.concatenate([s, snk], axis=-1), axis=-1)[..., :-1]
    else:
        p = jax.nn.softmax(s, axis=-1)
    o = jnp.einsum("bkgts,bskd->btkgd", p.astype(v.dtype), v)
    return o.reshape(o.shape[:2] + (-1,))

def diff_attend(q, k, v, lam, subln_gain, lam_init):
    s = jnp.einsum("btncd,bsncd->bncts", q, k).astype(jnp.float32) * (q.shape[-1] ** -0.5)
    p = jax.nn.softmax(s, axis=-1)
    a = p[:, :, 0] - lam * p[:, :, 1]
    o = jnp.einsum("bnts,bsne->btne", a.astype(v.dtype), v)
    o = rms_norm(o, subln_gain) * (1.0 - lam_init)
    return o.reshape(o.shape[:2] + (-1,))

def sweep_query_blocks(attend_block, q):
    n, length = q.shape[:2]
    nb = length // QBLOCK
    qb = jnp.moveaxis(q.reshape((n, nb, QBLOCK) + q.shape[2:]), 1, 0)
    o = lax.map(lambda a: attend_block(a[0], a[1]), (jnp.arange(nb), qb))
    return jnp.moveaxis(o, 0, 1).reshape(n, length, -1)

def windowed_latent(q, k_lat, v_lat, k_ctx, v_ctx, sink):
    length = k_lat.shape[1]
    span = QBLOCK + 2 * WINDOW
    pad = ((0, 0), (WINDOW, WINDOW), (0, 0), (0, 0))
    kp, vp = jnp.pad(k_lat, pad), jnp.pad(v_lat, pad)
    rel = jnp.arange(span)[None, :] - WINDOW - jnp.arange(QBLOCK)[:, None]
    band = jnp.abs(rel) <= WINDOW
    ctx_cols = jnp.ones((QBLOCK, k_ctx.shape[1]), dtype=bool)

    def block(b, qb):
        start = b * QBLOCK
        kb = lax.dynamic_slice_in_dim(kp, start, span, axis=1)
        vb = lax.dynamic_slice_in_dim(vp, start, span, axis=1)
        kpos = start - WINDOW + jnp.arange(span)
        valid = band & ((kpos >= 0) & (kpos < length))[None, :]
        mask = jnp.concatenate([valid, ctx_cols], axis=-1)
        return gqa_attend(qb, jnp.concatenate([kb, k_ctx], axis=1), jnp.concatenate([vb, v_ctx], axis=1), mask, sink)

    return sweep_query_blocks(block, q)

def merge_branches(ya, yb, yc, gates, P):
    g = jax.nn.sigmoid(gates.astype(jnp.float32)).astype(ya.dtype)
    ga, gb, gc = jnp.split(g, N_BRANCHES, axis=-1)
    m = ga * (ya @ P["w_branch_a"]) + gb * (yb @ P["w_branch_b"]) + gc * (yc @ P["w_branch_c"])
    return m @ P["w_out"]

def hier_moe(h, w_rg, w_re, w_gate, w_up, w_down):
    n = h.shape[0]
    g_logits = (h @ w_rg).astype(jnp.float32)
    g_prob = jax.nn.softmax(g_logits, axis=-1)
    g_idx = jnp.argmax(g_logits, axis=-1)
    g_w = jnp.take_along_axis(g_prob, g_idx[:, None], axis=-1)
    e_logits = (h @ w_re).astype(jnp.float32).reshape(n, N_GROUPS, EXPERTS_PER_GROUP)
    e_in_group = jnp.take_along_axis(e_logits, g_idx[:, None, None], axis=1)[:, 0]
    top_v, top_i = lax.top_k(e_in_group, TOP_K)
    w = jax.nn.softmax(top_v, axis=-1) * g_w
    flat_e = (g_idx[:, None] * EXPERTS_PER_GROUP + top_i).reshape(-1)
    order = jnp.argsort(flat_e)
    tok = order // TOP_K
    sizes = jnp.bincount(flat_e, length=N_EXPERTS).astype(jnp.int32)
    xs = h[tok]
    a = lax.ragged_dot(xs, w_gate, sizes)
    u = lax.ragged_dot(xs, w_up, sizes)
    y = lax.ragged_dot(jax.nn.silu(a) * u, w_down, sizes)
    y = y * w.reshape(-1)[order][:, None].astype(y.dtype)
    return jax.ops.segment_sum(y, tok, num_segments=n)

def hybrid_layer(l, x, ctx, silu_c, silu_c_ctx, P, rope, need_ctx):
    n, length, d = x.shape
    c_len = ctx.shape[1]
    mod = (silu_c @ P["w_ada"] + P["b_ada"]).reshape(n, N_MOD, 1, d)
    cmod = (silu_c_ctx @ P["w_ada"] + P["b_ada"]).reshape(N_MOD, 1, 1, d)
    lam_init = 0.8 - 0.6 * math.exp(-0.3 * l)
    lam = (jnp.exp(jnp.sum(P["lambda_q1"].astype(jnp.float32) * P["lambda_k1"].astype(jnp.float32)))
           - jnp.exp(jnp.sum(P["lambda_q2"].astype(jnp.float32) * P["lambda_k2"].astype(jnp.float32)))
           + lam_init)

    h = modulate(rms_norm(x), mod[:, 0], mod[:, 1])
    hc = modulate(rms_norm(ctx), cmod[0], cmod[1])
    proj = h @ P["w_in"]
    aq, bq, cq, gates = split_queries(proj[..., :Q_COLS], P, rope)
    ak, av, bk, bv, ck, cv = split_keys_values(proj[..., Q_COLS:], P, rope)
    if need_ctx:
        cproj = hc @ P["w_in"]
        ckv_in = cproj[..., Q_COLS:]
    else:
        ckv_in = hc @ P["w_in"][:, Q_COLS:]
    xak, xav, xbk, xbv, xck, xcv = split_keys_values(ckv_in, P, None)

    k_a, v_a = jnp.concatenate([ak, xak], axis=1), jnp.concatenate([av, xav], axis=1)
    k_b, v_b = jnp.concatenate([bk, xbk], axis=1), jnp.concatenate([bv, xbv], axis=1)
    ya = sweep_query_blocks(lambda b, qb: gqa_attend(qb, k_a, v_a), aq)
    yb = sweep_query_blocks(lambda b, qb: diff_attend(qb, k_b, v_b, lam, P["b_subln"], lam_init), bq)
    yc = windowed_latent(cq, ck, cv, xck, xcv, P["c_sink"])
    x = x + mod[:, 2] * merge_branches(ya, yb, yc, gates, P)

    if need_ctx:
        caq, cbq, ccq, cgates = split_queries(cproj[..., :Q_COLS], P, None)
        cya = gqa_attend(caq, xak, xav)
        cyb = diff_attend(cbq, xbk, xbv, lam, P["b_subln"], lam_init)
        cyc = gqa_attend(ccq, xck, xcv, sink=P["c_sink"])
        ctx = ctx + cmod[2] * merge_branches(cya, cyb, cyc, cgates, P)

    h2 = modulate(rms_norm(x), mod[:, 3], mod[:, 4])
    tokens = h2.reshape(n * length, d)
    if need_ctx:
        hc2 = modulate(rms_norm(ctx), cmod[3], cmod[4])
        tokens = jnp.concatenate([tokens, hc2.reshape(n * c_len, d)], axis=0)
    f = hier_moe(tokens, P["w_router_group"], P["w_router_expert"], P["w_exp_gate"], P["w_exp_up"], P["w_exp_down"])
    f = f.astype(x.dtype)
    x = x + mod[:, 5] * f[: n * length].reshape(n, length, d)
    if need_ctx:
        ctx = ctx + cmod[5] * f[n * length:].reshape(n, c_len, d)
    return x, ctx

def setup_inputs(seed: int = 0) -> dict:
    key = jax.random.key(seed)
    ks = jax.random.split(key, 28)
    f32 = jnp.float32
    nrm = lambda k, shape, s: jax.random.normal(k, shape, f32) * s
    gain = lambda k, shape: 1.0 + 0.05 * jax.random.normal(k, shape, f32)
    D = D_MODEL
    return {
        "x": nrm(ks[0], (BATCH, SEQ, D), 1.0),
        "c": nrm(ks[1], (BATCH, D), 1.0),
        "ctx": nrm(ks[2], (BATCH, CTX_LEN, D), 1.0),
        "c_ctx": nrm(ks[3], (D,), 1.0),
        "w_ada": nrm(ks[4], (DEPTH, D, N_MOD * D), 0.5 * D ** -0.5),
        "b_ada": nrm(ks[5], (DEPTH, N_MOD * D), 0.02),
        "w_in": nrm(ks[6], (DEPTH, D, IN_COLS), D ** -0.5),
        "a_qnorm": gain(ks[7], (DEPTH, HEAD_DIM)),
        "a_knorm": gain(ks[8], (DEPTH, HEAD_DIM)),
        "b_qnorm": gain(ks[9], (DEPTH, HEAD_DIM)),
        "b_knorm": gain(ks[10], (DEPTH, HEAD_DIM)),
        "c_qnorm": gain(ks[11], (DEPTH, HEAD_DIM)),
        "c_knorm": gain(ks[12], (DEPTH, HEAD_DIM)),
        "lambda_q1": nrm(ks[13], (DEPTH, HEAD_DIM), 0.1),
        "lambda_k1": nrm(ks[14], (DEPTH, HEAD_DIM), 0.1),
        "lambda_q2": nrm(ks[15], (DEPTH, HEAD_DIM), 0.1),
        "lambda_k2": nrm(ks[16], (DEPTH, HEAD_DIM), 0.1),
        "b_subln": gain(ks[17], (DEPTH, B_V_DIM)),
        "c_sink": nrm(ks[18], (DEPTH, C_HEADS), 0.5),
        "w_branch_a": nrm(ks[19], (DEPTH, A_WIDTH, D), A_WIDTH ** -0.5),
        "w_branch_b": nrm(ks[20], (DEPTH, B_WIDTH, D), B_WIDTH ** -0.5),
        "w_branch_c": nrm(ks[21], (DEPTH, C_WIDTH, D), C_WIDTH ** -0.5),
        "w_out": nrm(ks[22], (DEPTH, D, D), D ** -0.5),
        "w_router_group": nrm(ks[23], (DEPTH, D, N_GROUPS), D ** -0.5),
        "w_router_expert": nrm(ks[24], (DEPTH, D, N_EXPERTS), D ** -0.5),
        "w_exp_gate": nrm(ks[25], (DEPTH, N_EXPERTS, D, EXPERT_HIDDEN), D ** -0.5),
        "w_exp_up": nrm(ks[26], (DEPTH, N_EXPERTS, D, EXPERT_HIDDEN), D ** -0.5),
        "w_exp_down": nrm(ks[27], (DEPTH, N_EXPERTS, EXPERT_HIDDEN, D), EXPERT_HIDDEN ** -0.5),
    }

def reference(x, c, ctx, c_ctx, w_ada, b_ada, w_in, a_qnorm, a_knorm, b_qnorm, b_knorm, c_qnorm, c_knorm,
              lambda_q1, lambda_k1, lambda_q2, lambda_k2, b_subln, c_sink, w_branch_a, w_branch_b, w_branch_c,
              w_out, w_router_group, w_router_expert, w_exp_gate, w_exp_up, w_exp_down):
    rope = axial_rope_tables(x.shape[1])
    silu_c = jax.nn.silu(c)
    silu_c_ctx = jax.nn.silu(c_ctx)
    for l in range(DEPTH):
        P = {
            "w_ada": w_ada[l], "b_ada": b_ada[l], "w_in": w_in[l],
            "a_qnorm": a_qnorm[l], "a_knorm": a_knorm[l], "b_qnorm": b_qnorm[l], "b_knorm": b_knorm[l],
            "c_qnorm": c_qnorm[l], "c_knorm": c_knorm[l],
            "lambda_q1": lambda_q1[l], "lambda_k1": lambda_k1[l], "lambda_q2": lambda_q2[l], "lambda_k2": lambda_k2[l],
            "b_subln": b_subln[l], "c_sink": c_sink[l],
            "w_branch_a": w_branch_a[l], "w_branch_b": w_branch_b[l], "w_branch_c": w_branch_c[l], "w_out": w_out[l],
            "w_router_group": w_router_group[l], "w_router_expert": w_router_expert[l],
            "w_exp_gate": w_exp_gate[l], "w_exp_up": w_exp_up[l], "w_exp_down": w_exp_down[l],
        }
        x, ctx = hybrid_layer(l, x, ctx, silu_c, silu_c_ctx, P, rope, l < DEPTH - 1)
    return x


_drawn_inputs = setup_inputs


def setup_inputs(seed=0):
    import zlib

    import numpy as np

    out = dict(_drawn_inputs(seed))
    spreads = {}
    factors = {'a_qnorm': 8.0,
     'a_knorm': 8.0,
     'b_qnorm': 8.0,
     'b_knorm': 8.0,
     'c_qnorm': 8.0,
     'c_knorm': 8.0,
     'lambda_q1': 8.0,
     'lambda_k1': 8.0,
     'lambda_q2': 8.0,
     'lambda_k2': 8.0,
     'b_subln': 4.646,
     'c_sink': 8.0}
    for name, (base, spread) in spreads.items():
        noise = np.random.default_rng([zlib.crc32(name.encode()), seed]).standard_normal(out[name].shape)
        drawn = base * np.exp(spread * noise) if base else spread * noise
        out[name] = jnp.asarray(drawn.astype(out[name].dtype))
    for name, factor in factors.items():
        out[name] = (out[name] * factor).astype(out[name].dtype)
    return out
```

```python
from contextlib import ExitStack
import math

import numpy as np

import concourse.bass as bass
from concourse import mybir

P = 128
F32 = mybir.dt.float32
F32R = mybir.dt.float32r
BF16 = mybir.dt.bfloat16
I32 = mybir.dt.int32
U32 = mybir.dt.uint32
ALU = mybir.AluOpType
ACT = mybir.ActivationFunctionType
AX = mybir.AxisListType
ds = bass.ds

DEPTH, D, SEQ, CTX = 2, 1024, 1024, 256
T = SEQ + CTX
NT, NL = T // P, SEQ // P
KD = D // P
HD = 64
N_MOD = 6
EPS = 1e-6
NEG = -1e30
GRID_W, THETA = 64, 10000.0
A_Q, B_Q, C_Q, GATES = 0, 512, 1024, 1536
A_K, A_V, B_K, B_V, C_K, C_V = 4608, 4736, 4864, 5376, 5888, 6016
HALF = 256
QK_SLOTS = 36
SLOT_BK, SLOT_AK, SLOT_CK = 24, 32, 34
V_COLS = 768
NG, EG, NE, EH = 4, 8, 32, 512
MAX_JOBS = (2 * T // P + NE) // 2 * 2
Y_COLS = 3 * 512


class Event:

    def __init__(self, sem, slots=0, unit=1):
        self.sem, self.slots, self.unit = sem, slots, unit

    def done(self, g):
        return (g + (1 + self.slots)) * self.unit

    def free(self, g):
        return (g + 1) * self.unit

    def credit(self, eng):
        eng.sem_inc(self.sem, self.slots * self.unit)


def later(g, lag):
    return not isinstance(g, int) or g >= lag


def take_waits(eng, taken):
    eng.sem_inc(taken.sem, 1)


class Stage:
    whole_kernel = None

    def __init__(self, nc, name):
        self.nc, self.name, self.ctx, self.sems = nc, name, ExitStack(), []

    def __enter__(self):
        self.ctx.__enter__()
        return self

    def sb(self, name, shape, dt=F32, ctx=None):
        return (ctx or self.ctx).enter_context(self.nc.sbuf_tensor(f"{self.name}_{name}", shape, dt))

    def ps(self, name, shape, ctx=None):
        return (ctx or self.ctx).enter_context(self.nc.psum_tensor(f"{self.name}_{name}", shape, F32))

    def sem(self, name):
        s = self.ctx.enter_context(self.nc.semaphore(f"{self.name}_{name}"))
        self.sems.append(s)
        return s

    def event(self, name, slots=0):
        return Event(self.sem(name), slots)

    def dma(self, name, slots=0):
        return Event(self.sem(name), slots, 16)

    def pool_dma(self, name):
        return Event(Stage.whole_kernel.enter_context(self.nc.semaphore(f"{self.name}_{name}")), 0, 16)

    def __exit__(self, *a):
        if a[0] is None:
            nc, sems = self.nc, self.sems
            with nc.Block() as block:
                @block.sync
                def _(sp):
                    for s in sems:
                        sp.sem_clear(s)
        return self.ctx.__exit__(*a)


def stage_modulation(nc, io, scr):
    NC = N_MOD * D // 512
    with Stage(nc, "modulation") as st:
        cT = st.sb("cT", [P, KD, 2])
        sT = st.sb("sT", [P, KD, 2])
        w = [st.sb(f"w_ada{b}", [P, KD, 512]) for b in range(4)]
        bias = [st.sb(f"b_ada{b}", [2, 512]) for b in range(4)]
        row = [st.sb(f"mod_row{b}", [2, 512]) for b in range(4)]
        acc = [st.ps(f"mod_acc{b}", [P, 512]) for b in range(4)]
        c_in = st.dma("c_loaded")
        silu = st.event("silu_done")
        w_in = [st.dma(f"w_ada_loaded{b}") for b in range(4)]
        b_in = [st.dma(f"b_ada_loaded{b}") for b in range(4)]
        stored = [st.dma(f"mod_stored{b}", 1) for b in range(4)]
        mm = st.event("mod_products", 4)
        add = st.event("mod_bias_added", 4)
        with nc.Block() as block:
            @block.sync
            def _(sp):
                sp.dma_start(cT[:, :, :], io["c_cols"]).then_inc(c_in.sem, 16)
                with sp.Fori(0, NC // 2) as i:
                    for b in range(4):
                        l, n = b // 2, i * 2 + b % 2
                        sp.wait_ge(mm.sem, mm.free(i * 4 + b))
                        sp.dma_start(w[b][:, :, :], io["w_ada"][l].rearrange("(k p) n -> p k n", p=P)[
                            :, :, ds(n * 512, 512)]).then_inc(w_in[b].sem, 16)
                        sp.wait_ge(add.sem, add.free(i * 4 + b))
                        sp.dma_start(bias[b][:, :], io["b_ada"][l, ds(n * 512, 512)].partition_broadcast(2)
                                     ).then_inc(b_in[b].sem, 16)

            @block.scalar
            def _(act):
                for b in range(4):
                    stored[b].credit(act)
                act.wait_ge(c_in.sem, c_in.done(0))
                act.activation(sT[:, :, :], cT[:, :, :], ACT.Silu).then_inc(silu.sem, 1)
                with act.Fori(0, NC // 2) as i:
                    for b in range(4):
                        l, n = b // 2, i * 2 + b % 2
                        act.wait_ge(add.sem, add.done(i * 4 + b))
                        act.dma_start(scr["mod"][l, :, ds(n * 512, 512)], row[b][:, :]).then_inc(stored[b].sem, 16)
                for b in range(4):
                    act.wait_ge(stored[b].sem, stored[b].done(NC // 2 - 1))

            @block.tensor
            def _(pe):
                mm.credit(pe)
                pe.wait_ge(silu.sem, silu.done(0))
                with pe.Fori(0, NC // 2) as i:
                    for b in range(4):
                        pe.wait_ge(w_in[b].sem, w_in[b].done(i))
                        pe.wait_ge(add.sem, add.free(i * 4 + b))
                        for k in range(KD):
                            m = pe.matmul(acc[b][0:2, :], sT[:, k, :], w[b][:, k, :],
                                          start=(k == 0), stop=(k == KD - 1))
                        m.then_inc(mm.sem, 1)

            @block.vector
            def _(dve):
                add.credit(dve)
                with dve.Fori(0, NC // 2) as i:
                    for b in range(4):
                        dve.wait_ge(b_in[b].sem, b_in[b].done(i))
                        dve.wait_ge(mm.sem, mm.done(i * 4 + b))
                        dve.wait_ge(stored[b].sem, stored[b].free(i))
                        dve.tensor_tensor(row[b][:, :], acc[b][0:2, :], bias[b][:, :], ALU.add).then_inc(add.sem, 1)


def mod_rows(scr, l, j, dst, eng):
    return eng.dma_start(dst, scr["mod"][l, :, j * D:(j + 1) * D].partition_broadcast(P))


def stream_rows(io, scr, l, t):
    if l:
        return scr["x2"][ds(t * P, P), :]
    if isinstance(t, int) and t >= NL:
        return io["ctx"][0, ds((t - NL) * P, P), :]
    return io["x"][0, ds(t * P, P), :]


def stage_project(nc, io, scr, l, nq):
    with Stage(nc, f"project{l}") as st:
        ident = st.sb("ident", [P, P])
        hT = st.sb("hT", [P, 2, KD, T], F32R)
        const_in = st.dma("ident_loaded")
        with ExitStack() as inner:
            norm_transposed(nc, io, scr, l, st, inner, ident, hT, const_in)
        with ExitStack() as inner:
            project_heads(nc, io, scr, l, nq, st, inner, ident, hT)


def norm_transposed(nc, io, scr, l, st, inner, ident, hT, const_in):
    def sb(name, shape, dt=F32):
        return st.sb(name, shape, dt, inner)

    shift = sb("shift_rows", [P, 2, D])
    scale = sb("scale_rows", [P, 2, D])
    x = [sb(f"x_tile{b}", [P, D]) for b in range(2)]
    h = [sb(f"h_tile{b}", [P, D]) for b in range(2)]
    square = sb("square", [P, D])
    stat = sb("norm_stat", [P, 2, 4])
    acc = [st.ps(f"hT_acc{b}", [P, D], inner) for b in range(2)]
    x_in = [st.dma(f"x_loaded{b}") for b in range(2)]
    rows_in, sq, ms, rt, rs, plus1, sc, hd = (
        st.dma("mod_rows_loaded"), st.event("squares"), st.event("mean_square"), st.event("root"),
        st.event("rstd"), st.event("scale_plus_1"), st.event("scaled"), st.event("h_ready"))
    tr, hi, lo = st.event("h_transposed"), st.event("hT_hi"), st.event("hT_lo")

    def pairs(eng, body):
        body(0, 0)
        with eng.Fori(1, NL // 2) as p:
            body(p, 0)
        body(NL // 2, 1)

    with nc.Block() as block:
        @block.sync
        def _(sp):
            sp.dma_start(ident[:, :], io["k_ident"]).then_inc(const_in.sem, 16)
            mod_rows(scr, l, 0, shift[:, :, :], sp).then_inc(rows_in.sem, 16)
            mod_rows(scr, l, 1, scale[:, :, :], sp).then_inc(rows_in.sem, 16)

            def body(p, who):
                for b in range(2):
                    t = p * 2 + b
                    if later(t, 2):
                        sp.wait_ge(sc.sem, sc.done(t - 2))
                    sp.dma_start(x[b][:, :], stream_rows(io, scr, l, t)).then_inc(x_in[b].sem, 16)
            pairs(sp, body)

        @block.scalar
        def _(act):
            def split_hi(t, b):
                act.wait_ge(tr.sem, tr.done(t))
                act.copy(hT[:, 0, :, ds(t * P, P)], acc[b][:, :].rearrange("p (k n) -> p k n", k=KD)
                         ).then_inc(hi.sem, 1)

            def body(p, who):
                for b in range(2):
                    t = p * 2 + b
                    act.wait_ge(x_in[b].sem, x_in[b].done(p))
                    act.activation(square[:, :], x[b][:, :], ACT.Square,
                                   accum_out=stat[:, b, 0:1]).then_inc(sq.sem, 1)
                    act.wait_ge(ms.sem, ms.done(t))
                    act.activation(stat[:, b, 2:3], stat[:, b, 1:2], ACT.Sqrt).then_inc(rt.sem, 1)
                    if not isinstance(t, int) or t > 0:
                        split_hi(t - 1, 1 - b)
            pairs(act, body)
            split_hi(NT - 1, 1)

        @block.vector
        def _(dve):
            dve.wait_ge(rows_in.sem, rows_in.done(1))
            dve.tensor_scalar(scale[:, :, :], scale[:, :, :], 1.0, None, ALU.add).then_inc(plus1.sem, 1)
            dve.wait_ge(plus1.sem, plus1.done(0))

            def split_lo(t, b):
                dve.wait_ge(hi.sem, hi.done(t))
                to = hT[:, :, :, ds(t * P, P)]
                dve.tensor_tensor(to[:, 1], acc[b][:, :].rearrange("p (k n) -> p k n", k=KD),
                                  to[:, 0].bitcast(F32), ALU.subtract).then_inc(lo.sem, 1)

            def body(p, who):
                for b in range(2):
                    t = p * 2 + b
                    dve.wait_ge(sq.sem, sq.done(t))
                    dve.tensor_scalar(stat[:, b, 1:2], stat[:, b, 0:1], 1.0 / D, EPS, ALU.mult, ALU.add
                                      ).then_inc(ms.sem, 1)
                    dve.wait_ge(rt.sem, rt.done(t))
                    dve.reciprocal(stat[:, b, 3:4], stat[:, b, 2:3]).then_inc(rs.sem, 1)
                    dve.wait_ge(rs.sem, rs.done(t))
                    if later(t, 2):
                        dve.wait_ge(tr.sem, tr.done(t - 2))
                    dve.scalar_tensor_tensor(out=h[b][:, :], in0=x[b][:, :], scalar=stat[:, b, 3:4],
                                             in1=scale[:, who, :], op0=ALU.mult, op1=ALU.mult).then_inc(sc.sem, 1)
                    dve.wait_ge(sc.sem, sc.done(t))
                    dve.tensor_tensor(h[b][:, :], h[b][:, :], shift[:, who, :], ALU.add).then_inc(hd.sem, 1)
                    if not isinstance(t, int) or t > 0:
                        split_lo(t - 1, 1 - b)
            pairs(dve, body)
            split_lo(NT - 1, 1)

        @block.tensor
        def _(pe):
            pe.wait_ge(const_in.sem, const_in.done(0))

            def body(p, who):
                for b in range(2):
                    t = p * 2 + b
                    pe.wait_ge(hd.sem, hd.done(t))
                    if later(t, 2):
                        pe.wait_ge(lo.sem, lo.done(t - 2))
                    for k in range(KD):
                        m = pe.transpose(acc[b][:, ds(k * P, P)], h[b][:, k * P:(k + 1) * P], ident[:, :])
                    m.then_inc(tr.sem, 1)
            pairs(pe, body)


def project_heads(nc, io, scr, l, nq, st, inner, ident, hT):
    def sb(name, shape, dt=F32):
        return st.sb(name, shape, dt, inner)

    w_raw = [sb(f"w_raw{b}", [P, KD, HALF]) for b in range(2)]
    w_split = [sb(f"w_split{b}", [P, 2, KD, HALF], F32R) for b in range(2)]
    table = sb("rope_table", [P, 6, NL + 1, 2, HD])
    rope = sb("rope", [P, NL + 1, 2, HD])
    gain = sb("gains", [P, 6, HD])
    square = [sb(f"square{b}", [P, HALF]) for b in range(2)]
    normed = [sb(f"normed{b}", [P, HALF]) for b in range(2)]
    by_cos = [sb(f"by_cos{b}", [P, HALF]) for b in range(2)]
    by_sin = [sb(f"by_sin{b}", [P, HALF]) for b in range(2)]
    turned = [sb(f"turned{b}", [P, HALF]) for b in range(2)]
    halves = [sb(f"halves{b}", [P, 4, 2, HD], F32R) for b in range(2)]
    staged = [sb(f"staged{b}", [P, 4, P], F32R) for b in range(2)]
    v_staged = [sb(f"v_staged{b}", [P, HALF]) for b in range(2)]
    stat = sb("head_stat", [P, 2, 4, 4])
    acc = [st.ps(f"proj_acc{b}", [P, 512], inner) for b in range(4)]
    turn = [st.ps(f"turn_acc{b}", [P, 512], inner) for b in range(2)]

    raw_in = [st.dma(f"w_in_loaded{b}") for b in range(2)]
    tab_in, hT_out = st.dma("rope_loaded"), st.dma("hT_stored")
    tab, w_hi, w_lo = st.event("rope_tables"), st.event("w_hi"), st.event("w_lo")
    mm, sq, ss, ms, rt, rs = (st.event("projected"), st.event("head_squares"), st.event("head_sums"),
                              st.event("head_mean_squares"), st.event("head_roots"), st.event("head_rstd"))
    y, cs, sn, tn, hh, hl = (st.event("head_normed"), st.event("times_cos"), st.event("times_sin"),
                             st.event("rotated"), st.event("head_hi"), st.event("head_lo"))
    taken = st.event("pool_waits_taken")
    tr, ev, v_ev = st.event("head_transposed"), st.event("head_staged"), st.event("values_staged")
    qk_out = [st.dma(f"heads_stored{b}") for b in range(2)]
    v_out = [st.dma(f"values_stored{b}") for b in range(2)]

    NQ2, NT2 = 2 * nq, 2 * NT
    n_norm = 3 * NQ2 + NT2 + NT
    KINDS = ("a_qnorm", "b_qnorm", "c_qnorm", "b_knorm", "a_knorm", "c_knorm")

    def steps(p):
        return NQ2 if not isinstance(p, int) or p < 3 else NT2

    def first(p):
        return p * NQ2 if not isinstance(p, int) or p < 3 else 3 * NQ2 + (p - 3) * NT2

    def lagged(p, s):
        return (p, s) if s >= 0 else (p - 1, s + steps(p - 1))

    def is_value(p, s):
        return isinstance(p, int) and (p == 5 or (p == 4 and s >= NT))

    def tile_of(p, s):
        return s % (steps(p) // 2)

    def pairs(eng, body):
        body(0)
        with eng.Fori(1, 3) as p:
            body(p)
        for p in range(3, 6):
            body(p)

    def uses(p, s):
        return (p * nq if not isinstance(p, int) or p < 3 else 3 * nq + (p - 3) * NT) + s // 2

    def exists(p):
        return not isinstance(p, int) or 0 <= p <= 5

    def heads(buf, h0, h1):
        return buf[:, h0 * HD:h1 * HD].rearrange("p (h d) -> p h d", d=HD)

    def kinds(p, s):
        if isinstance(p, int) and p == 4:
            return [(0, 2, 4), (2, 4, 5)]
        return [(0, 4, p)]

    def table_of(kind, p, s, which, n):
        row = min(tile_of(p, s), NL)
        if isinstance(kind, int):
            tb = table[:, kind, row, which, :]
        else:
            tb = table[:, ds(kind, 1), row, which, :].rearrange("p o d -> p (o d)")
        return tb.unsqueeze(1).to_broadcast([P, n, HD])

    w_in = io["w_heads"][l].rearrange("(k p) n -> p k n", p=P)

    with nc.Block() as block:
        @block.sync
        def _(sp):
            sp.dma_start(rope[:, :, :, :], io["k_rope"].rearrange("t p c d -> p t c d")).then_inc(tab_in.sem, 16)
            for n, kind in enumerate(KINDS):
                sp.dma_start(gain[:, n, :], io[kind][l].partition_broadcast(P)).then_inc(tab_in.sem, 16)

            def load(p, hf):
                if later(p * 2 + hf, 2):
                    sp.wait_ge(w_lo.sem, w_lo.done(p * 2 + hf - 2))
                sp.dma_start(w_raw[hf][:, :, :], w_in[:, :, ds((p * 2 + hf) * HALF, HALF)]
                             ).then_inc(raw_in[hf].sem, 16)

            def store(p, s):
                g, b, t = first(p) + s, s % 2, tile_of(p, s)
                if is_value(p, s):
                    sp.wait_ge(v_ev.sem, v_ev.done(g - n_norm))
                    col = (p - 5) * 512 + 256 + (s // NT) * HALF if p == 5 else 0
                    sp.dma_start(scr["v"][t * P:(t + 1) * P, col:col + HALF], v_staged[b][:, :]
                                 ).then_inc(v_out[b].sem, 16)
                    return
                sp.wait_ge(ev.sem, ev.done(g))
                if isinstance(p, int) and p == 4:
                    slot = SLOT_AK
                else:
                    slot = p * 8 + (s // (steps(p) // 2)) * 4
                sp.dma_start(scr["qk"][ds(slot, 4), :, t * P:(t + 1) * P].rearrange("h p n -> p h n"),
                             staged[b][:, :, :].bitcast(F32)).then_inc(qk_out[b].sem, 16)

            load(0, 0)
            load(0, 1)
            sp.dma_start(scr["hT"].rearrange("c p k n -> p c k n"), hT[:, :, :, :].bitcast(F32)).then_inc(hT_out.sem, 16)

            def body(p):
                for s in range(steps(p)):
                    if s in (3, 6) and exists(p + 1):
                        load(p + 1, s // 6)
                    q, r = lagged(p, s - 3)
                    if exists(q):
                        store(q, r)
            pairs(sp, body)
            for s in range(NT2 - 3, NT2):
                store(5, s)
            sp.wait_ge(hT_out.sem, hT_out.done(0))
            for b in range(2):
                sp.wait_ge(qk_out[b].sem, qk_out[b].done(n_norm // 2 - 1))
                sp.wait_ge(v_out[b].sem, v_out[b].done((3 * NT) // 2 - 1))

        @block.scalar
        def _(act):
            def split(p, hf):
                act.wait_ge(raw_in[hf].sem, raw_in[hf].done(p))
                if not isinstance(p, int) or p > 0:
                    act.wait_ge(mm.sem, mm.done(first(p - 1) + (hf + 1) * steps(p - 1) // 2 - 1))
                act.copy(w_split[hf][:, 0, :, :], w_raw[hf][:, :, :]).then_inc(w_hi.sem, 1)

            def stage_heads(p, s):
                g, b = first(p) + s, s % 2
                act.wait_ge(tr.sem, tr.done(g))
                if later(uses(p, s), 1):
                    act.wait_ge(qk_out[b].sem, qk_out[b].done(uses(p, s) - 1))
                act.copy(staged[b][:, :, :], turn[b][:, :].rearrange("p (h n) -> p h n", h=4)).then_inc(ev.sem, 1)

            def round_heads(p, s):
                g, b = first(p) + s, s % 2
                act.wait_ge(tn.sem, tn.done(g))
                if later(g, 2):
                    act.wait_ge(tr.sem, tr.done(g - 2))
                act.copy(halves[b][:, :, 0, :], turned[b][:, :].rearrange("p (h d) -> p h d", h=4)
                         ).then_inc(hh.sem, 1)

            def body(p):
                for s in range(steps(p)):
                    g, b = first(p) + s, s % 2
                    if s == 2:
                        split(p, 1)
                    if s == steps(p) // 2 + 2 and exists(p + 1):
                        split(p + 1, 0)
                    q, r = lagged(p, s - 2)
                    lag = exists(q) and not is_value(q, r)
                    if is_value(p, s):
                        q1, r1 = lagged(p, s - 1)
                        if not is_value(q1, r1):
                            round_heads(q1, r1)
                        if lag:
                            stage_heads(q, r)
                        act.wait_ge(mm.sem, mm.done(g))
                        if later(uses(p, s) - n_norm // 2, 1):
                            act.wait_ge(v_out[b].sem, v_out[b].done(uses(p, s) - n_norm // 2 - 1))
                        act.copy(v_staged[b][:, :], acc[s % 4][:, 0:HALF]).then_inc(v_ev.sem, 1)
                        continue
                    act.wait_ge(mm.sem, mm.done(g))
                    if later(g, 2):
                        act.wait_ge(ss.sem, ss.done(g - 2))
                    act.activation(square[b][:, :], acc[s % 4][:, 0:HALF], ACT.Square).then_inc(sq.sem, 1)
                    act.wait_ge(ms.sem, ms.done(g))
                    act.activation(stat[:, b, 2, :], stat[:, b, 1, :], ACT.Sqrt).then_inc(rt.sem, 1)
                    q1, r1 = lagged(p, s - 1)
                    if exists(q1):
                        round_heads(q1, r1)
                    if lag:
                        stage_heads(q, r)
            split(0, 0)
            pairs(act, body)

        @block.vector
        def _(dve):
            def split(p, hf):
                dve.wait_ge(w_hi.sem, w_hi.done(p * 2 + hf))
                dve.tensor_tensor(w_split[hf][:, 1, :, :], w_raw[hf][:, :, :],
                                  w_split[hf][:, 0, :, :].bitcast(F32), ALU.subtract).then_inc(w_lo.sem, 1)

            def turn_heads(p, s):
                g, b = first(p) + s, s % 2
                dve.wait_ge(cs.sem, cs.done(g))
                dve.wait_ge(sn.sem, sn.done(g))
                if later(g, 2):
                    dve.wait_ge(hl.sem, hl.done(g - 2))
                dve.tensor_tensor(turned[b][:, :], by_cos[b][:, :], by_sin[b][:, :], ALU.add).then_inc(tn.sem, 1)

            def body(p):
                for s in range(steps(p)):
                    g, b = first(p) + s, s % 2
                    if s == 2:
                        split(p, 1)
                    if s == steps(p) // 2 + 2 and exists(p + 1):
                        split(p + 1, 0)
                    q, r = lagged(p, s - 1)
                    if is_value(p, s):
                        if not is_value(q, r):
                            turn_heads(q, r)
                        continue
                    dve.wait_ge(sq.sem, sq.done(g))
                    dve.tensor_reduce(stat[:, b, 0, :], square[b][:, :].rearrange("p (h d) -> p h d", h=4),
                                      AX.X, ALU.add).then_inc(ss.sem, 1)
                    dve.wait_ge(ss.sem, ss.done(g))
                    dve.tensor_scalar(stat[:, b, 1, :], stat[:, b, 0, :], 1.0 / HD, EPS, ALU.mult, ALU.add
                                      ).then_inc(ms.sem, 1)
                    if exists(q):
                        turn_heads(q, r)
                    dve.wait_ge(rt.sem, rt.done(g))
                    dve.reciprocal(stat[:, b, 3, :], stat[:, b, 2, :]).then_inc(rs.sem, 1)
                    dve.wait_ge(rs.sem, rs.done(g))
                    if later(g, 2):
                        dve.wait_ge(sn.sem, sn.done(g - 2))
                    dve.tensor_tensor(normed[b][:, :].rearrange("p (h d) -> p h d", h=4),
                                      acc[s % 4][:, 0:HALF].rearrange("p (h d) -> p h d", h=4),
                                      stat[:, b, 3, :].unsqueeze(2).to_broadcast([P, 4, HD]), ALU.mult
                                      ).then_inc(y.sem, 1)
                    dve.wait_ge(y.sem, y.done(g))
                    for n, (h0, h1, kind) in enumerate(kinds(p, s)):
                        o = dve.tensor_tensor(heads(by_cos[b], h0, h1), heads(normed[b], h0, h1),
                                              table_of(kind, p, s, 0, h1 - h0), ALU.mult)
                    o.then_inc(cs.sem, 1)
            split(0, 0)
            dve.wait_ge(tab.sem, tab.done(6 * 3 - 1))
            pairs(dve, body)

        @block.gpsimd
        def _(pool):
            pool.wait_ge(tab_in.sem, tab_in.done(6))
            for n in range(6):
                for which, d0, g0, w in ((0, 0, 0, HD), (1, 0, HD // 2, HD // 2), (1, HD // 2, 0, HD // 2)):
                    pool.tensor_tensor(table[:, n, :, which, d0:d0 + w], rope[:, :, which, d0:d0 + w],
                                       gain[:, n, g0:g0 + w].unsqueeze(1).to_broadcast([P, NL + 1, w]), ALU.mult
                                       ).then_inc(tab.sem, 1)
            pool.wait_ge(tab.sem, tab.done(6 * 3 - 1))

            def rest_of_heads(p, s):
                g, b = first(p) + s, s % 2
                pool.wait_ge(hh.sem, hh.done(g))
                pool.tensor_tensor(halves[b][:, :, 1, :], turned[b][:, :].rearrange("p (h d) -> p h d", h=4),
                                   halves[b][:, :, 0, :].bitcast(F32), ALU.subtract).then_inc(hl.sem, 1)

            def body(p):
                for s in range(steps(p)):
                    q, r = lagged(p, s - 1)
                    if is_value(p, s):
                        if not is_value(q, r):
                            rest_of_heads(q, r)
                        continue
                    g, b = first(p) + s, s % 2
                    pool.wait_ge(y.sem, y.done(g))
                    if later(g, 2):
                        pool.wait_ge(tn.sem, tn.done(g - 2))
                    take_waits(pool, taken)
                    for h0, h1, kind in kinds(p, s):
                        for half_ in range(2):
                            src = heads(normed[b], h0, h1)[:, :, (1 - half_) * 32:(1 - half_) * 32 + 32]
                            o = pool.tensor_tensor(heads(by_sin[b], h0, h1)[:, :, half_ * 32:half_ * 32 + 32], src,
                                                   table_of(kind, p, s, 1, h1 - h0)[:, :, half_ * 32:half_ * 32 + 32],
                                                   ALU.mult)
                    o.then_inc(sn.sem, 1)
                    if exists(q):
                        rest_of_heads(q, r)
            pairs(pool, body)

        @block.tensor
        def _(pe):
            def transposes(p, s):
                g, b = first(p) + s, s % 2
                pe.wait_ge(hl.sem, hl.done(g))
                pe.wait_ge(hh.sem, hh.done(g))
                if later(g, 2):
                    pe.wait_ge(ev.sem, ev.done(g - 2))
                for h in range(4):
                    m = pe.transpose(turn[b][:, h * P:(h + 1) * P],
                                     halves[b][:, h, :, :].rearrange("p c d -> p (c d)").bitcast(F32), ident[:, :])
                m.then_inc(tr.sem, 1)

            def body(p):
                for s in range(steps(p)):
                    g, t, hf = first(p) + s, tile_of(p, s), s // (steps(p) // 2)
                    if t == 0:
                        pe.wait_ge(w_lo.sem, w_lo.done(p * 2 + hf))
                    if is_value(p, s) and g - n_norm >= 4:
                        pe.wait_ge(v_ev.sem, v_ev.done(g - n_norm - 4))
                    else:
                        if later(g, 4):
                            pe.wait_ge(y.sem, y.done(g - 4))
                    for i, (a, c) in enumerate(((0, 0), (0, 1), (1, 0))):
                        for k in range(KD):
                            m = pe.matmul(acc[s % 4][:, 0:HALF], hT[:, a, k, t * P:(t + 1) * P],
                                          w_split[hf][:, c, k, :], start=(i == 0 and k == 0),
                                          stop=(i == 2 and k == KD - 1))
                    m.then_inc(mm.sem, 1)
                    q, r = lagged(p, s - 2)
                    if exists(q) and not is_value(q, r):
                        transposes(q, r)
            pairs(pe, body)


SCORE_SCALE = HD ** -0.5


class Step:

    def __init__(self, t, banded):
        self.t = t
        if t >= NL:
            self.runs, self.col0 = [(0, NL, NT - NL)], 0
        elif banded:
            a, b = max(t - 1, 0), min(t + 2, NL)
            self.col0 = 512 - (b - a) * P
            self.runs = [(self.col0, a, b - a), (512, NL, NT - NL)]
        else:
            self.col0 = 0
            self.runs = [(c * P, c, min(4, NT - c)) for c in range(0, NT, 4)]
        self.tiles = [a + i for _, a, n in self.runs for i in range(n)]
        self.n = len(self.tiles)
        self.cols = slice(self.col0, self.col0 + self.n * P)
        self.by_act = self.n if self.n <= 4 else (self.n - 1) // 4 * 4
        self.mask0 = (1 if t == 0 else 0) if banded and t < NL else None


def stage_attend_gqa(nc, io, scr, l, nq, banded):
    q_slot, k_slot, v_col, y_col = (16, SLOT_CK, P, 2 * 512) if banded else (0, SLOT_AK, 0, 0)
    NS = 2 * nq
    with Stage(nc, f"attend_{'c' if banded else 'a'}{l}") as st:
        ident = st.sb("ident", [P, P])
        keys = [st.sb(f"keys{b}", [P, 2, T], F32R) for b in range(2)]
        queries = [st.sb(f"queries{b}", [P, T], F32R) for b in range(2)]
        values = [st.sb(f"values{b}", [P, NT, HD]) for b in range(2)]
        probs = [st.sb(f"probs{b}", [P, T]) for b in range(2)]
        probsT = [st.sb(f"probsT{b}", [P, NT, P]) for b in range(2)]
        out = [st.sb(f"out{b}", [P, nq, HD]) for b in range(2)]
        stat = st.sb("stat", [P, 4, 8])
        scores = [st.ps(f"scores{b}", [P, 1536]) for b in range(2)]
        acc = [st.ps(f"out_acc{b}", [P, 512]) for b in range(2)]
        const_in = st.dma("constants_loaded")
        k_in, q_in, v_in, y_out = ([st.dma(f"{n}{b}") for b in range(2)] for n in (
            "keys_loaded", "queries_loaded", "values_loaded", "out_stored"))
        qk, mx, nb, ex = st.event("scores_done"), st.event("row_max"), st.event("bias_ready"), st.event("exp_done")
        tr, ca, cv = st.event("probs_transposed"), st.event("copied_by_act"), st.event("copied_by_dve")
        pv, sm, rc, yd = (st.event("values_summed"), st.event("denominator"), st.event("reciprocal"),
                          st.event("out_ready"))
        const_split = st.event("constants_rounded")
        if banded:
            ident_r, band_r = st.sb("ident_r", [P, P], F32R), st.sb("band_r", [P, 3, P], F32R)
            band = st.sb("band", [P, 3, P])
            sink = st.sb("sink", [P, 8])
            neg_sink = st.sb("neg_sink", [P, 8])
            es = st.event("exp_of_sink")
        steps = [Step(s % nq, banded) for s in range(NS)]

        n_dve = sum(sx.n > sx.by_act for sx in steps)

        def by_dve(i, s):
            if steps[s].n > steps[s].by_act:
                return i * n_dve + sum(sx.n > sx.by_act for sx in steps[:s])

        def wait_copied(eng, i, s):
            if exists(i):
                eng.wait_ge(ca.sem, ca.done(i * NS + s))
                if by_dve(i, s) is not None:
                    eng.wait_ge(cv.sem, cv.done(by_dve(i, s)))

        def before(i, s):
            return (i, s) if s >= 0 else (i - 1, s + NS)

        def exists(i):
            return not isinstance(i, int) or i >= 0

        def bodies(eng, body):
            body(0)
            with eng.Fori(1, 4) as i:
                body(i)

        clear_results = not banded and l == 0
        if clear_results:
            zeros, zeroed = st.sb("zeros", [P, D]), st.event("zeros_ready")
            cleared = st.pool_dma("results_cleared")

        with nc.Block() as block:
            if clear_results:
                @block.gpsimd
                def _(pool):
                    pool.memset(zeros[:, :], 0.0).then_inc(zeroed.sem, 1)
                    pool.wait_ge(zeroed.sem, zeroed.done(0))
                    with pool.Fori(0, MAX_JOBS) as j:
                        pool.dma_start(scr["ye"][ds(j * P, P), :], zeros[:, :]).then_inc(cleared.sem, 16)
                    pool.wait_ge(cleared.sem, cleared.done(MAX_JOBS - 1))

            @block.sync
            def _(sp):
                sp.dma_start(ident[:, :], io["k_ident"]).then_inc(const_in.sem, 16)
                if banded:
                    sp.dma_start(band[:, :, :], io["k_band"]).then_inc(const_in.sem, 16)
                    sp.dma_start(sink[:, :], io["c_sink"][l].partition_broadcast(P)).then_inc(const_in.sem, 16)

                def load(i, b):
                    if not isinstance(i, int) or i > 0:
                        sp.wait_ge(qk.sem, qk.done((i - 1) * NS + (b + 1) * nq - 1))
                    for half in range(2):
                        for rep in range(2):
                            sp.dma_start(keys[b][rep * HD:(rep + 1) * HD, half, :].bitcast(F32),
                                         scr["qk"][ds(i // 2 + k_slot, 1), half * HD:(half + 1) * HD, :].rearrange(
                                             "o p n -> (o p) n")).then_inc(k_in[b].sem, 16)
                    sp.dma_start(queries[b][:, :].bitcast(F32),
                                 scr["qk"][ds(i * 2 + b + q_slot, 1), :, :].rearrange("o p n -> (o p) n")
                                 ).then_inc(q_in[b].sem, 16)
                    if not isinstance(i, int) or i > 0:
                        sp.wait_ge(pv.sem, pv.done((i - 1) * NS + (b + 1) * nq - 1))
                    sp.dma_start(values[b][:, :, :], scr["v"].rearrange("(t p) n -> p t n", p=P)[
                        :, :, ds(v_col + (i // 2) * HD, HD)]).then_inc(v_in[b].sem, 16)

                def store(i, b):
                    sp.wait_ge(yd.sem, yd.done(i * NS + (b + 1) * nq - 1))
                    sp.dma_start(scr["y"][0:nq * P, :].rearrange("(t p) n -> p t n", p=P)[
                        :, :, ds(y_col + (i * 2 + b) * HD, HD)], out[b][:, :, :]).then_inc(y_out[b].sem, 16)

                load(0, 0)
                load(0, 1)

                def body(i):
                    if exists(i - 1):
                        store(i - 1, 1)
                        load(i, 1)
                    store(i, 0)
                    if not isinstance(i, int) or i < 3:
                        load(i + 1, 0)
                body(0)
                with sp.Fori(1, 3) as i:
                    body(i)
                body(3)
                store(3, 1)
                for b in range(2):
                    sp.wait_ge(y_out[b].sem, y_out[b].done(3))

            @block.tensor
            def _(pe):
                def transposes(i, s):
                    g, b, sx = i * NS + s, s % 2, steps[s]
                    pe.wait_ge(ex.sem, ex.done(g))
                    for j in range(sx.n):
                        m = pe.transpose(scores[b][:, j * P:(j + 1) * P], probs[b][:, j * P:(j + 1) * P], ident[:, :])
                    m.then_inc(tr.sem, 1)

                def sum_values(i, s):
                    g, b, sx, hb = i * NS + s, s % 2, steps[s], s // nq
                    wait_copied(pe, i, s)
                    if later(g, 2):
                        pe.wait_ge(yd.sem, yd.done(g - 2))
                    if s % nq == 0:
                        pe.wait_ge(v_in[hb].sem, v_in[hb].done(i))
                    for j, kt in enumerate(sx.tiles):
                        m = pe.matmul(acc[b][:, 0:HD], probsT[b][:, j, :], values[hb][:, kt, :],
                                      start=(j == 0), stop=(j == sx.n - 1))
                    m.then_inc(pv.sem, 1)

                def body(i):
                    for s in range(NS):
                        g, b, hb, sx = i * NS + s, s % 2, s // nq, steps[s]
                        if s % nq == 0:
                            pe.wait_ge(k_in[hb].sem, k_in[hb].done(i * 4 + 3))
                            pe.wait_ge(q_in[hb].sem, q_in[hb].done(i))
                        wait_copied(pe, *before(i, s - 2))
                        for col, a, n in sx.runs:
                            masked = sx.mask0 is not None and a < NL
                            for half in range(2):
                                m = pe.matmul(scores[b][:, col:col + n * P], queries[hb][:, sx.t * P:(sx.t + 1) * P],
                                              keys[hb][:, half, a * P:(a + n) * P], start=(half == 0),
                                              stop=(half == 1 and not masked))
                            if masked:
                                m = pe.matmul(scores[b][:, col:col + n * P], ident_r[:, :],
                                              band_r[:, sx.mask0:sx.mask0 + n, :].rearrange("p t n -> p (t n)"),
                                              start=False, stop=True)
                        m.then_inc(qk.sem, 1)
                        q, r = before(i, s - 1)
                        if exists(q):
                            transposes(q, r)
                        q, r = before(i, s - 2)
                        if exists(q):
                            sum_values(q, r)
                pe.wait_ge(const_in.sem, const_in.done(2 if banded else 0))
                if banded:
                    pe.wait_ge(const_split.sem, const_split.done(1))
                bodies(pe, body)
                transposes(3, NS - 1)
                sum_values(3, NS - 2)
                sum_values(3, NS - 1)

            @block.scalar
            def _(act):
                def copy_out(i, s):
                    g, b, n = i * NS + s, s % 2, steps[s].by_act
                    act.wait_ge(tr.sem, tr.done(g))
                    if later(g, 2):
                        act.wait_ge(pv.sem, pv.done(g - 2))
                    act.copy(probsT[b][:, 0:n, :], scores[b][:, 0:n * P].rearrange("p (j n) -> p j n", n=P)
                             ).then_inc(ca.sem, 1)

                def body(i):
                    for s in range(NS):
                        g, b, sx = i * NS + s, s % 2, steps[s]
                        q, r = before(i, s - 1)
                        if exists(q):
                            copy_out(q, r)
                        act.wait_ge(nb.sem, nb.done(g))
                        if later(g, 2):
                            act.wait_ge(tr.sem, tr.done(g - 2))
                        act.activation(probs[b][:, 0:sx.n * P], scores[b][:, sx.cols], ACT.Exp, scale=SCORE_SCALE,
                                       bias=stat[:, s % 4, 1:2], accum_out=stat[:, s % 4, 2:3]).then_inc(ex.sem, 1)
                        if banded:
                            act.activation(stat[:, s % 4, 4:5], sink[:, ds(i * 2 + s // nq, 1)], ACT.Exp,
                                           bias=stat[:, s % 4, 1:2]).then_inc(es.sem, 1)
                if banded:
                    act.wait_ge(const_in.sem, const_in.done(2))
                bodies(act, body)
                copy_out(3, NS - 1)

            @block.vector
            def _(dve):
                def copy_out(i, s):
                    g, b, n, n1 = i * NS + s, s % 2, steps[s].by_act, steps[s].n
                    if n == n1:
                        return
                    dve.wait_ge(tr.sem, tr.done(g))
                    if later(g, 2):
                        dve.wait_ge(pv.sem, pv.done(g - 2))
                    dve.tensor_copy(probsT[b][:, n:n1, :], scores[b][:, n * P:n1 * P].rearrange(
                        "p (j n) -> p j n", n=P)).then_inc(cv.sem, 1)

                def finish(i, s):
                    g, b, hb, k = i * NS + s, s % 2, s // nq, s % 4
                    if banded:
                        dve.wait_ge(es.sem, es.done(g))
                        dve.tensor_tensor(stat[:, k, 5:6], stat[:, k, 2:3], stat[:, k, 4:5], ALU.add
                                          ).then_inc(sm.sem, 1)
                        dve.wait_ge(sm.sem, sm.done(g))
                    total = 5 if banded else 2
                    dve.reciprocal(stat[:, k, 3:4], stat[:, k, total:total + 1]).then_inc(rc.sem, 1)
                    dve.wait_ge(rc.sem, rc.done(g))
                    dve.wait_ge(pv.sem, pv.done(g))
                    if s % nq == 0 and exists(i - 1):
                        dve.wait_ge(y_out[hb].sem, y_out[hb].done(i - 1))
                    dve.tensor_scalar(out[hb][:, s % nq, :], acc[b][:, 0:HD], stat[:, k, 3:4], None, ALU.mult
                                      ).then_inc(yd.sem, 1)

                def body(i):
                    for s in range(NS):
                        g, b, k, sx = i * NS + s, s % 2, s % 4, steps[s]
                        dve.wait_ge(qk.sem, qk.done(g))
                        dve.tensor_reduce(stat[:, k, 0:1], scores[b][:, sx.cols], AX.X, ALU.max).then_inc(mx.sem, 1)
                        dve.wait_ge(mx.sem, mx.done(g))
                        if banded:
                            dve.tensor_scalar(stat[:, k, 1:2], stat[:, k, 0:1], -SCORE_SCALE,
                                              neg_sink[:, ds(i * 2 + s // nq, 1)], ALU.mult, ALU.min
                                              ).then_inc(nb.sem, 1)
                        else:
                            dve.tensor_scalar(stat[:, k, 1:2], stat[:, k, 0:1], -SCORE_SCALE, None, ALU.mult
                                              ).then_inc(nb.sem, 1)
                        q, r = before(i, s - 1)
                        if exists(q):
                            copy_out(q, r)
                        q, r = before(i, s - 2)
                        if exists(q):
                            finish(q, r)
                if banded:
                    dve.wait_ge(const_in.sem, const_in.done(2))
                    dve.tensor_copy(ident_r[:, :], ident[:, :]).then_inc(const_split.sem, 1)
                    dve.tensor_copy(band_r[:, :, :], band[:, :, :]).then_inc(const_split.sem, 1)
                    dve.tensor_scalar(neg_sink[:, :], sink[:, :], -1.0, None, ALU.mult).then_inc(const_split.sem, 1)
                    dve.wait_ge(const_split.sem, const_split.done(2))
                bodies(dve, body)
                copy_out(3, NS - 1)
                finish(3, NS - 2)
                finish(3, NS - 1)


def stage_attend_a(nc, io, scr, l, nq):
    stage_attend_gqa(nc, io, scr, l, nq, banded=False)


def stage_attend_c(nc, io, scr, l, nq):
    stage_attend_gqa(nc, io, scr, l, nq, banded=True)


def lambda_init(l):
    return 0.8 - 0.6 * math.exp(-0.3 * l)


def stage_attend_b(nc, io, scr, l, nq):
    NH, VD = 4, 2 * HD
    with Stage(nc, f"attend_b{l}") as st:
        ident = st.sb("ident", [P, P])
        keys = st.sb("keys", [P, 2, 2, 2, T], F32R)
        values = st.sb("values", [P, 2, NT, VD])
        out = st.sb("out", [P, 2, nq, VD])
        queries = st.sb("queries", [P, 2, T], F32R)
        p0 = [st.sb(f"p0_{b}", [P, T]) for b in range(2)]
        p1 = [st.sb(f"p1_{b}", [P, T]) for b in range(2)]
        probsT = [st.sb(f"probsT{b}", [P, NT, P]) for b in range(2)]
        lam_in = st.sb("lambda_vectors", [P, 4, HD])
        lam_mul = st.sb("lambda_products", [P, 2, HD])
        lam = st.sb("lambda", [P, 8])
        stat = st.sb("stat", [P, 2, 12])
        scores = [st.ps(f"scores{b}", [P, 1536]) for b in range(2)]
        acc = [st.ps(f"out_acc{b}", [P, 512]) for b in range(2)]
        const_in, lam_ld = st.dma("constants_loaded"), st.dma("lambdas_loaded")
        k_in, v_in, y_out = st.dma("keys_loaded"), st.dma("values_loaded"), st.dma("out_stored", 2)
        q_in = [st.dma(f"queries_loaded{b}") for b in range(2)]
        qk = [st.event(f"scores_done{c}") for c in range(2)]
        mx = [st.event(f"row_max{c}") for c in range(2)]
        nb = [st.event(f"bias_ready{c}") for c in range(2)]
        ex = [st.event(f"exp_done{c}") for c in range(2)]
        lm, cf, df, tr, ca, pv, rc, yd = (
            st.event("lambda_step"), st.event("coefficient_step"), st.event("difference"),
            st.event("probs_transposed"), st.event("copied_out"), st.event("values_summed"),
            st.event("reciprocal"), st.event("out_ready"))
        dd, p1_scaled = st.event("difference_by_dve"), st.event("p1_scaled")
        taken = st.event("pool_waits_taken")
        steps = [Step(t, False) for t in range(nq)]

        def before(n, s):
            return (n, s) if s >= 0 else (n - 1, s + nq)

        def exists(n):
            return not isinstance(n, int) or n >= 0

        def heads(eng, body):
            body(0)
            with eng.Fori(1, NH) as n:
                body(n)

        with nc.Block() as block:
            @block.sync
            def _(sp):
                sp.dma_start(ident[:, :], io["k_ident"]).then_inc(const_in.sem, 16)
                for j, name in enumerate(("lambda_q1", "lambda_q2", "lambda_k1", "lambda_k2")):
                    sp.dma_start(lam_in[:, j, :], io[name][l].partition_broadcast(P)).then_inc(lam_ld.sem, 16)

                def load_kv(n, par, prev):
                    if prev is not None:
                        sp.wait_ge(qk[1].sem, qk[1].done(prev * nq + nq - 1))
                    for half in range(2):
                        for rep in range(2):
                            for c in range(2):
                                sp.dma_start(keys[rep * HD:(rep + 1) * HD, ds(par, 1), c, half, :].rearrange(
                                                 "p o n -> p (o n)").bitcast(F32),
                                             scr["qk"][ds(n * 2 + (SLOT_BK + c), 1), half * HD:(half + 1) * HD, :
                                                       ].rearrange("o p n -> (o p) n")).then_inc(k_in.sem, 16)
                    if prev is not None:
                        sp.wait_ge(pv.sem, pv.done(prev * nq + nq - 1))
                    sp.dma_start(values[:, ds(par, 1), :, :].rearrange("p o t n -> p (o t) n"),
                                 scr["v"].rearrange("(t p) n -> p t n", p=P)[:, :, ds(n * VD + 2 * P, VD)]
                                 ).then_inc(v_in.sem, 16)

                def load_q(n, half):
                    a, b = (0, nq // 2 * P) if half == 0 else (nq // 2 * P, nq * P)
                    if not isinstance(n, int) or n > 0:
                        sp.wait_ge(qk[1].sem, qk[1].done((n - 1) * nq + b // P - 1))
                    sp.dma_start(queries[:, :, a:b].bitcast(F32), scr["qk"][ds(n * 2 + 8, 2), :, a:b].rearrange(
                        "c p n -> p c n")).then_inc(q_in[half].sem, 16)

                def store(n):
                    sp.wait_ge(yd.sem, yd.done(n * nq + nq - 1))
                    sp.dma_start(scr["y"][0:nq * P, :].rearrange("(t p) n -> p t n", p=P)[
                        :, :, ds(512 + n * VD, VD)],
                        out[:, ds(n % 2, 1), :, :].rearrange("p o t n -> p (o t) n")).then_inc(y_out.sem, 16)
                y_out.credit(sp)
                load_kv(0, 0, None)
                load_q(0, 0)
                load_q(0, 1)
                load_kv(1, 1, None)
                load_q(1, 0)
                load_q(1, 1)
                store(0)
                with sp.Fori(2, NH) as n:
                    load_kv(n, n % 2, n - 2)
                    load_q(n, 0)
                    load_q(n, 1)
                    store(n - 1)
                store(NH - 1)
                sp.wait_ge(y_out.sem, y_out.done(NH - 1))

            @block.tensor
            def _(pe):
                def transposes(n, s):
                    g, b, sx = n * nq + s, s % 2, steps[s]
                    pe.wait_ge(df.sem, df.done(g))
                    pe.wait_ge(dd.sem, dd.done(g))
                    if not isinstance(g, int) or g < NH * nq - 1:
                        pe.wait_ge(ex[0].sem, ex[0].done(g + 1))
                    else:
                        pe.wait_ge(ex[1].sem, ex[1].done(g - 1))
                    for j in range(sx.n):
                        m = pe.transpose(scores[1 - b][:, j * P:(j + 1) * P], p0[b][:, j * P:(j + 1) * P], ident[:, :])
                    m.then_inc(tr.sem, 1)

                def sum_values(n, s):
                    g, b, sx = n * nq + s, s % 2, steps[s]
                    pe.wait_ge(ca.sem, ca.done(g))
                    if later(g, 2):
                        pe.wait_ge(yd.sem, yd.done(g - 2))
                    if s == 0:
                        pe.wait_ge(v_in.sem, v_in.done(n))
                    for j, kt in enumerate(sx.tiles):
                        v = values[:, ds(n % 2, 1), kt, :].rearrange("p o n -> p (o n)")
                        m = pe.matmul(acc[b][:, 0:VD], probsT[b][:, j, :], v, start=(j == 0), stop=(j == sx.n - 1))
                    m.then_inc(pv.sem, 1)

                def score(n, s, c):
                    sx = steps[s]
                    for col, a, w in sx.runs:
                        for half in range(2):
                            k = keys[:, ds(n % 2, 1), c, half, a * P:(a + w) * P].rearrange("p o n -> p (o n)")
                            m = pe.matmul(scores[(s + c) % 2][:, col:col + w * P], queries[:, c, sx.t * P:(sx.t + 1) * P], k,
                                          start=(half == 0), stop=(half == 1))
                    m.then_inc(qk[c].sem, 1)

                def body(n):
                    for s in range(nq):
                        g = n * nq + s
                        if s == 0:
                            pe.wait_ge(k_in.sem, k_in.done(n * 8 + 7))
                        if s in (0, nq // 2):
                            pe.wait_ge(q_in[s // (nq // 2)].sem, q_in[s // (nq // 2)].done(n))
                        if later(g, 1):
                            pe.wait_ge(ex[1].sem, ex[1].done(g - 1))
                        score(n, s, 0)
                        if later(g, 2):
                            pe.wait_ge(ca.sem, ca.done(g - 2))
                        score(n, s, 1)
                        q, r = before(n, s - 2)
                        if exists(q):
                            sum_values(q, r)
                        q, r = before(n, s - 1)
                        if exists(q):
                            transposes(q, r)
                pe.wait_ge(const_in.sem, const_in.done(0))
                heads(pe, body)
                sum_values(NH - 1, nq - 2)
                transposes(NH - 1, nq - 1)
                sum_values(NH - 1, nq - 1)

            @block.scalar
            def _(act):
                def copy_out(n, s):
                    g, b, w = n * nq + s, s % 2, steps[s].n
                    act.wait_ge(tr.sem, tr.done(g))
                    if later(g, 2):
                        act.wait_ge(pv.sem, pv.done(g - 2))
                    act.copy(probsT[b][:, 0:w, :], scores[1 - b][:, 0:w * P].rearrange("p (j n) -> p j n", n=P)
                             ).then_inc(ca.sem, 1)

                def exps(n, s, c, to):
                    g, k, sx = n * nq + s, s % 2, steps[s]
                    act.wait_ge(nb[c].sem, nb[c].done(g))
                    act.activation(to[:, 0:sx.n * P], scores[(s + c) % 2][:, sx.cols], ACT.Exp, scale=SCORE_SCALE,
                                   bias=stat[:, k, 2 + c:3 + c], accum_out=stat[:, k, 4 + c:5 + c]
                                   ).then_inc(ex[c].sem, 1)

                def body(n):
                    for s in range(nq):
                        g = n * nq + s
                        if later(g, 2):
                            act.wait_ge(tr.sem, tr.done(g - 2))
                        exps(n, s, 0, p0[s % 2])
                        if later(g, 2):
                            act.wait_ge(df.sem, df.done(g - 2))
                            act.wait_ge(dd.sem, dd.done(g - 2))
                        exps(n, s, 1, p1[s % 2])
                        q, r = before(n, s - 1)
                        if exists(q):
                            copy_out(q, r)
                act.wait_ge(lm.sem, lm.done(1))
                act.activation(lam[:, 2:4], lam[:, 0:2], ACT.Exp).then_inc(lm.sem, 1)
                heads(act, body)
                copy_out(NH - 1, nq - 1)

            @block.vector
            def _(dve):
                def row_max(n, s, c):
                    g, k, sx = n * nq + s, s % 2, steps[s]
                    dve.wait_ge(qk[c].sem, qk[c].done(g))
                    dve.tensor_reduce(stat[:, k, c:c + 1], scores[(s + c) % 2][:, sx.cols], AX.X, ALU.max).then_inc(mx[c].sem, 1)
                    dve.wait_ge(mx[c].sem, mx[c].done(g))
                    dve.tensor_scalar(stat[:, k, 2 + c:3 + c], stat[:, k, c:c + 1], -SCORE_SCALE, None, ALU.mult
                                      ).then_inc(nb[c].sem, 1)

                def coefficients(n, s):
                    g, k = n * nq + s, s % 2
                    dve.wait_ge(ex[1].sem, ex[1].done(g))
                    dve.wait_ge(ex[0].sem, ex[0].done(g))
                    dve.reciprocal(stat[:, k, 6:7], stat[:, k, 5:6]).then_inc(cf.sem, 1)
                    if later(g, 2):
                        dve.wait_ge(yd.sem, yd.done(g - 2))
                    dve.reciprocal(stat[:, k, 8:9], stat[:, k, 4:5]).then_inc(cf.sem, 1)
                    dve.wait_ge(cf.sem, cf.done(g * 3))
                    dve.tensor_scalar(stat[:, k, 7:8], stat[:, k, 4:5], stat[:, k, 6:7], lam[:, 5:6],
                                      ALU.mult, ALU.mult).then_inc(cf.sem, 1)
                    w = steps[s].n // 2 * P
                    dve.wait_ge(cf.sem, cf.done(g * 3 + 2))
                    dve.scalar_tensor_tensor(out=p0[k][:, 0:w], in0=p1[k][:, 0:w], scalar=stat[:, k, 7:8],
                                             in1=p0[k][:, 0:w], op0=ALU.mult, op1=ALU.add).then_inc(dd.sem, 1)

                def finish(n, s):
                    g, b = n * nq + s, s % 2
                    dve.wait_ge(pv.sem, pv.done(g))
                    if s == 0:
                        dve.wait_ge(y_out.sem, y_out.free(n))
                    dve.tensor_scalar(out[:, ds(n % 2, 1), s, :].rearrange("p o n -> p (o n)"), acc[b][:, 0:VD],
                                      stat[:, b, 8:9], None, ALU.mult).then_inc(yd.sem, 1)

                def body(n):
                    for s in range(nq):
                        q, r = before(n, s - 1)
                        if exists(q):
                            coefficients(q, r)
                        row_max(n, s, 0)
                        row_max(n, s, 1)
                        q, r = before(n, s - 2)
                        if exists(q):
                            finish(q, r)
                dve.wait_ge(lam_ld.sem, lam_ld.done(3))
                dve.tensor_tensor(lam_mul[:, :, :], lam_in[:, 0:2, :], lam_in[:, 2:4, :], ALU.mult).then_inc(lm.sem, 1)
                dve.wait_ge(lm.sem, lm.done(0))
                dve.tensor_reduce(lam[:, 0:2], lam_mul[:, :, :], AX.X, ALU.add).then_inc(lm.sem, 1)
                dve.wait_ge(lm.sem, lm.done(2))
                dve.tensor_tensor(lam[:, 4:5], lam[:, 3:4], lam[:, 2:3], ALU.subtract).then_inc(lm.sem, 1)
                dve.wait_ge(lm.sem, lm.done(3))
                dve.tensor_scalar(lam[:, 5:6], lam[:, 4:5], -lambda_init(l), None, ALU.add).then_inc(lm.sem, 1)
                dve.wait_ge(lm.sem, lm.done(4))
                heads(dve, body)
                coefficients(NH - 1, nq - 1)
                finish(NH - 1, nq - 2)
                finish(NH - 1, nq - 1)

            @block.gpsimd
            def _(pool):
                def body(n):
                    for s in range(nq):
                        g, k, a, w = n * nq + s, s % 2, steps[s].n // 2 * P, steps[s].n * P
                        pool.wait_ge(cf.sem, cf.done(g * 3 + 2))
                        take_waits(pool, taken)
                        pool.tensor_scalar(p1[k][:, a:w], p1[k][:, a:w], stat[:, k, 7:8], None, ALU.mult
                                           ).then_inc(p1_scaled.sem, 1)
                        pool.wait_ge(p1_scaled.sem, p1_scaled.done(g))
                        pool.tensor_tensor(p0[k][:, a:w], p0[k][:, a:w], p1[k][:, a:w], ALU.add
                                           ).then_inc(df.sem, 1)
                heads(pool, body)


def stage_merge(nc, io, scr, l, nq):
    KB = 4
    YK = 3 * KB
    KU = KD + KB
    chunks = [(0, 4), (4, 4)] + ([(8, 2)] if nq > NL else [])
    UC = 3 * KD
    with Stage(nc, f"merge{l}") as st:
        ident = st.sb("ident", [P, P])
        hT = st.sb("hT", [P, 2, KD, 512], F32R)
        yT = st.sb("yT", [P, 2, YK, 512], F32R)
        y = [st.sb(f"y{i}", [P, Y_COLS]) for i in range(4)]
        gain = st.sb("subln_gain", [P, 2 * HD])
        square = st.sb("square", [P, 512])
        stat = st.sb("stat", [P, 4, 4])
        w_raw = [st.sb(f"w_raw{b}", [P, KU, P]) for b in range(3)]
        w_split = [st.sb(f"w_split{b}", [P, 2, KU, P], F32R) for b in range(3)]
        gate = [st.sb(f"gate{b}", [P, 512]) for b in range(3)]
        part = st.sb("part", [P, 512])
        m_sum = st.sb("m_sum", [P, 512])
        m_split = st.sb("m_split", [P, 2, 512], F32R)
        acc = st.ps("acc", [P, 6, 512])
        const_in, h_in, m_out = st.dma("constants_loaded"), st.dma("hT_loaded"), st.dma("mT_stored")
        y_in = [st.dma(f"y_loaded{i}") for i in range(4)]
        w_in = [st.dma(f"w_loaded{b}") for b in range(3)]
        sq, ss, ms, rt, rs, nr, gn = (st.event(n) for n in (
            "b_squares", "b_sums", "b_mean_squares", "b_roots", "b_rstd", "b_normed", "b_scaled"))
        g1, tr, yh, yl = (st.event(n) for n in ("gain_scaled", "y_transposed", "yT_hi", "yT_lo"))
        wh, wl, mg, mb, sg, pt, sm, mh, ml = (st.event(n) for n in (
            "w_hi", "w_lo", "gate_products", "branch_products", "gate_ready", "gated_branch", "branch_added",
            "m_hi", "m_lo"))
        i_of, n_tiles = [], 0
        for _, n in chunks:
            i_of.append(n_tiles)
            n_tiles += n

        def units(eng, c, body):
            body(c, 0)
            with eng.Fori(1, KD - 1) as f:
                body(c, f)
            body(c, KD - 1)

        def unit(c, f, b):
            return (f + c * KD) * 3 + b

        def ahead(c, f, b, n):
            b += n
            f, b = f + b // 3, b % 3
            if isinstance(f, int) and f >= KD:
                c, f = c + 1, f - KD
            return c, f, b

        with nc.Block() as block:
            @block.sync
            def _(sp):
                def load_w(c, f, b):
                    if c < len(chunks):
                        if later(unit(c, f, b), 3):
                            sp.wait_ge(wl.sem, wl.done(unit(c, f, b) - 3))
                        sp.dma_start(w_raw[b][:, :, :].rearrange("p k n -> p (k n)"),
                                     io["w_merge"][l][ds(f, 1), b, :, :, :].rearrange("o p k n -> p (o k n)")
                                     ).then_inc(w_in[b].sem, 16)

                def load_tokens(c):
                    t0, n = chunks[c]
                    for i in range(n):
                        if c > 0:
                            sp.wait_ge(tr.sem, tr.done(i_of[c - 1] + i))
                        sp.dma_start(y[i][:, :], scr["y"][(t0 + i) * P:(t0 + i + 1) * P, :]).then_inc(y_in[i].sem, 16)
                    if c > 0:
                        sp.wait_ge(mg.sem, mg.done(unit(c, 0, 0) - 1))
                    for half in range(2):
                        sp.dma_start(hT[:, half, :, 0:n * P].bitcast(F32),
                                     scr["hT"][half, :, :, t0 * P:(t0 + n) * P]).then_inc(h_in.sem, 16)

                def body(c, f):
                    t0, n = chunks[c]
                    for b in range(3):
                        load_w(*ahead(c, f, b, 3))
                    sp.wait_ge(ml.sem, ml.done(f + c * KD))
                    sp.dma_start(scr["mT"].rearrange("c p k n -> p c k n")[:, :, ds(f, 1), t0 * P:(t0 + n) * P
                                                                              ].rearrange("p c o n -> p c (o n)"),
                                 m_split[:, :, 0:n * P].bitcast(F32)).then_inc(m_out.sem, 16)
                sp.dma_start(ident[:, :], io["k_ident"]).then_inc(const_in.sem, 16)
                sp.dma_start(gain[:, :], io["b_subln"][l].partition_broadcast(P)).then_inc(const_in.sem, 16)
                for b in range(3):
                    load_w(0, 0, b)
                for c in range(len(chunks)):
                    load_tokens(c)
                    units(sp, c, body)
                sp.wait_ge(m_out.sem, m_out.done(len(chunks) * KD - 1))

            @block.scalar
            def _(act):
                def split(c, f, b):
                    if c < len(chunks):
                        act.wait_ge(w_in[b].sem, w_in[b].done(f + c * KD))
                        if later(unit(c, f, b), 3):
                            act.wait_ge(mb.sem, mb.done(unit(c, f, b) - 3))
                        act.copy(w_split[b][:, 0, :, :], w_raw[b][:, :, :]).then_inc(wh.sem, 1)

                def prepare(c):
                    for i in range(chunks[c][1]):
                        n = i_of[c] + i
                        act.wait_ge(y_in[i].sem, y_in[i].done(c))
                        if later(n, 1):
                            act.wait_ge(ss.sem, ss.done(n - 1))
                        act.activation(square[:, :], y[i][:, 512:1024], ACT.Square).then_inc(sq.sem, 1)
                        act.wait_ge(ms.sem, ms.done(n))
                        act.activation(stat[:, 2, :], stat[:, 1, :], ACT.Sqrt).then_inc(rt.sem, 1)
                        if i:
                            copy_hi(c, i - 1)
                    copy_hi(c, chunks[c][1] - 1)

                def copy_hi(c, i):
                    n = i_of[c] + i
                    act.wait_ge(tr.sem, tr.done(n))
                    act.copy(yT[:, 0, :, i * P:(i + 1) * P],
                             acc[:, (n % 2) * 3:(n % 2) * 3 + 3, :].rearrange("p b (j n) -> p (b j) n", n=P)
                             ).then_inc(yh.sem, 1)

                def body(c, f):
                    w = chunks[c][1] * P
                    for b in range(3):
                        u = unit(c, f, b)
                        split(*ahead(c, f, b, 2))
                        act.wait_ge(mg.sem, mg.done(u))
                        if later(u, 3):
                            act.wait_ge(pt.sem, pt.done(u - 3))
                        act.activation(gate[b][:, 0:w], acc[:, b, 0:w], ACT.Sigmoid).then_inc(sg.sem, 1)
                    act.wait_ge(sm.sem, sm.done((f + c * KD) * 2 + 1))
                    if not isinstance(f, int) or f + c * KD > 0:
                        act.wait_ge(m_out.sem, m_out.done(f + c * KD - 1))
                    act.copy(m_split[:, 0, 0:w], m_sum[:, 0:w]).then_inc(mh.sem, 1)
                split(0, 0, 0)
                split(0, 0, 1)
                for c in range(len(chunks)):
                    prepare(c)
                    units(act, c, body)

            @block.vector
            def _(dve):
                def split(c, f, b):
                    if c < len(chunks):
                        dve.wait_ge(wh.sem, wh.done(unit(c, f, b)))
                        dve.tensor_tensor(w_split[b][:, 1, :, :], w_raw[b][:, :, :],
                                          w_split[b][:, 0, :, :].bitcast(F32), ALU.subtract).then_inc(wl.sem, 1)

                def prepare(c):
                    for i in range(chunks[c][1]):
                        n = i_of[c] + i
                        dve.wait_ge(sq.sem, sq.done(n))
                        dve.tensor_reduce(stat[:, 0, :], square[:, :].rearrange("p (h d) -> p h d", h=4), AX.X,
                                          ALU.add).then_inc(ss.sem, 1)
                        dve.wait_ge(ss.sem, ss.done(n))
                        dve.tensor_scalar(stat[:, 1, :], stat[:, 0, :], 1.0 / (2 * HD), EPS, ALU.mult, ALU.add
                                          ).then_inc(ms.sem, 1)
                        dve.wait_ge(rt.sem, rt.done(n))
                        dve.reciprocal(stat[:, 3, :], stat[:, 2, :]).then_inc(rs.sem, 1)
                        dve.wait_ge(rs.sem, rs.done(n))
                        yb = y[i][:, 512:1024].rearrange("p (h d) -> p h d", h=4)
                        dve.tensor_tensor(yb, yb, stat[:, 3, :].unsqueeze(2).to_broadcast([P, 4, 2 * HD]), ALU.mult
                                          ).then_inc(nr.sem, 1)
                        dve.wait_ge(nr.sem, nr.done(n))
                        dve.tensor_tensor(yb, yb, gain[:, :].unsqueeze(1).to_broadcast([P, 4, 2 * HD]), ALU.mult
                                          ).then_inc(gn.sem, 1)
                        if i:
                            copy_lo(c, i - 1)
                    copy_lo(c, chunks[c][1] - 1)

                def copy_lo(c, i):
                    n = i_of[c] + i
                    dve.wait_ge(yh.sem, yh.done(n))
                    dve.tensor_tensor(yT[:, 1, :, i * P:(i + 1) * P],
                                      acc[:, (n % 2) * 3:(n % 2) * 3 + 3, :].rearrange("p b (j n) -> p (b j) n", n=P),
                                      yT[:, 0, :, i * P:(i + 1) * P].bitcast(F32), ALU.subtract).then_inc(yl.sem, 1)

                def body(c, f):
                    w = chunks[c][1] * P
                    for b in range(3):
                        u = unit(c, f, b)
                        split(*ahead(c, f, b, 2))
                        dve.wait_ge(sg.sem, sg.done(u))
                        dve.wait_ge(mb.sem, mb.done(u))
                        if b == 0:
                            if not isinstance(f, int) or f + c * KD > 0:
                                dve.wait_ge(ml.sem, ml.done(f + c * KD - 1))
                            dve.tensor_tensor(m_sum[:, 0:w], gate[b][:, 0:w], acc[:, 3 + b, 0:w], ALU.mult
                                              ).then_inc(pt.sem, 1)
                            continue
                        dve.tensor_tensor(part[:, 0:w], gate[b][:, 0:w], acc[:, 3 + b, 0:w], ALU.mult
                                          ).then_inc(pt.sem, 1)
                        dve.wait_ge(pt.sem, pt.done(u))
                        dve.tensor_tensor(m_sum[:, 0:w], m_sum[:, 0:w], part[:, 0:w], ALU.add).then_inc(sm.sem, 1)
                        dve.wait_ge(sm.sem, sm.done((f + c * KD) * 2 + b - 1))
                    dve.wait_ge(mh.sem, mh.done(f + c * KD))
                    dve.tensor_tensor(m_split[:, 1, 0:w], m_sum[:, 0:w], m_split[:, 0, 0:w].bitcast(F32),
                                      ALU.subtract).then_inc(ml.sem, 1)
                split(0, 0, 0)
                split(0, 0, 1)
                dve.wait_ge(const_in.sem, const_in.done(1))
                dve.tensor_scalar(gain[:, :], gain[:, :], 1.0 - lambda_init(l), None, ALU.mult).then_inc(g1.sem, 1)
                dve.wait_ge(g1.sem, g1.done(0))
                for c in range(len(chunks)):
                    prepare(c)
                    units(dve, c, body)

            @block.tensor
            def _(pe):
                def body(c, f):
                    w = chunks[c][1] * P
                    for b in range(3):
                        u = unit(c, f, b)
                        pe.wait_ge(wl.sem, wl.done(u))
                        if later(u, 3):
                            pe.wait_ge(pt.sem, pt.done(u - 3))
                        for bank, act_T, k0, n in ((b, hT, 0, KD), (3 + b, yT, KD, KB)):
                            for i, (a, x) in enumerate(((0, 0), (0, 1), (1, 0))):
                                for k in range(n):
                                    kk = k if act_T is hT else b * KB + k
                                    m = pe.matmul(acc[:, bank, 0:w], w_split[b][:, a, k0 + k, :],
                                                  act_T[:, x, kk, 0:w], start=(i == 0 and k == 0),
                                                  stop=(i == 2 and k == n - 1))
                            m.then_inc(mg.sem if act_T is hT else mb.sem, 1)
                pe.wait_ge(const_in.sem, const_in.done(1))
                for c in range(len(chunks)):
                    for i in range(chunks[c][1]):
                        n = i_of[c] + i
                        pe.wait_ge(gn.sem, gn.done(n))
                        if c and i < 2:
                            pe.wait_ge(pt.sem, pt.done(unit(c, 0, 0) - 1))
                        if i >= 2:
                            pe.wait_ge(yl.sem, yl.done(n - 2))
                        for j in range(YK):
                            bank = (n % 2) * 3 + j // 4
                            m = pe.transpose(acc[:, bank, (j % 4) * P:(j % 4 + 1) * P], y[i][:, j * P:(j + 1) * P],
                                             ident[:, :])
                        m.then_inc(tr.sem, 1)
                    pe.wait_ge(h_in.sem, h_in.done(c * 2 + 1))
                    pe.wait_ge(yl.sem, yl.done(i_of[c] + chunks[c][1] - 1))
                    units(pe, c, body)


def stage_output(nc, io, scr, l, nq):
    with Stage(nc, f"output{l}") as st:
        w_raw = [st.sb(f"w_raw{b}", [P, D]) for b in range(2)]
        w = st.sb("w_out", [P, 2, KD, D], F32R)
        gate = st.sb("gate_rows", [P, 2, D])
        mT = [st.sb(f"mT{b}", [P, 2, KD, P], F32R) for b in range(2)]
        x = [st.sb(f"x{b}", [P, D]) for b in range(2)]
        o = [st.sb(f"o{b}", [P, D]) for b in range(2)]
        acc = [st.ps(f"acc{b}", [P, D]) for b in range(2)]
        rows_in = st.dma("gate_loaded")
        w_in, m_in, x_in = ([st.dma(f"{n}{b}") for b in range(2)] for n in ("w_loaded", "mT_loaded", "x_loaded"))
        out = [st.dma(f"x1_stored{b}") for b in range(2)]
        wh, wl, mm, gd, ad = (st.event(n) for n in ("w_hi", "w_lo", "products", "gated", "added"))

        def pairs(eng, body):
            body(0, 0)
            with eng.Fori(1, NL // 2) as p:
                body(p, 0)
            if nq > NL:
                body(NL // 2, 1)

        with nc.Block() as block:
            @block.sync
            def _(sp):
                for k in range(KD):
                    if later(k, 2):
                        sp.wait_ge(wl.sem, wl.done(k - 2))
                    sp.dma_start(w_raw[k % 2][:, :], io["w_out"][l, k * P:(k + 1) * P, :]).then_inc(w_in[k % 2].sem, 16)
                mod_rows(scr, l, 2, gate[:, :, :], sp).then_inc(rows_in.sem, 16)

                def body(p, who):
                    for b in range(2):
                        t = p * 2 + b
                        if later(t, 2):
                            sp.wait_ge(mm.sem, mm.done(t - 2))
                        for half in range(2):
                            sp.dma_start(mT[b][:, half, :, :].bitcast(F32), scr["mT"][half, :, :, ds(t * P, P)]
                                         ).then_inc(m_in[b].sem, 16)
                        if later(t, 2):
                            sp.wait_ge(ad.sem, ad.done(t - 2))
                        sp.dma_start(x[b][:, :], stream_rows(io, scr, l, t)).then_inc(x_in[b].sem, 16)
                pairs(sp, body)

            @block.scalar
            def _(act):
                for k in range(KD):
                    act.wait_ge(w_in[k % 2].sem, w_in[k % 2].done(k // 2))
                    act.copy(w[:, 0, k, :], w_raw[k % 2][:, :]).then_inc(wh.sem, 1)

                def body(p, who):
                    for b in range(2):
                        act.wait_ge(ad.sem, ad.done(p * 2 + b))
                        act.dma_start(scr["x1"][ds((p * 2 + b) * P, P), :], o[b][:, :]).then_inc(out[b].sem, 16)
                pairs(act, body)
                for b in range(2):
                    act.wait_ge(out[b].sem, out[b].done(nq // 2 - 1))

            @block.vector
            def _(dve):
                for k in range(KD):
                    dve.wait_ge(wh.sem, wh.done(k))
                    dve.tensor_tensor(w[:, 1, k, :], w_raw[k % 2][:, :], w[:, 0, k, :].bitcast(F32), ALU.subtract
                                      ).then_inc(wl.sem, 1)
                dve.wait_ge(rows_in.sem, rows_in.done(0))

                def body(p, who):
                    for b in range(2):
                        t = p * 2 + b
                        dve.wait_ge(mm.sem, mm.done(t))
                        if later(p, 1):
                            dve.wait_ge(out[b].sem, out[b].done(p - 1))
                        dve.tensor_tensor(o[b][:, :], acc[b][:, :], gate[:, who, :], ALU.mult).then_inc(gd.sem, 1)
                        dve.wait_ge(gd.sem, gd.done(t))
                        dve.wait_ge(x_in[b].sem, x_in[b].done(p))
                        dve.tensor_tensor(o[b][:, :], o[b][:, :], x[b][:, :], ALU.add).then_inc(ad.sem, 1)
                pairs(dve, body)

            @block.tensor
            def _(pe):
                def body(p, who):
                    for b in range(2):
                        t = p * 2 + b
                        pe.wait_ge(m_in[b].sem, m_in[b].done(p * 2 + 1))
                        if later(t, 2):
                            pe.wait_ge(gd.sem, gd.done(t - 2))
                        if isinstance(t, int) and t == 0:
                            pe.wait_ge(wl.sem, wl.done(KD - 1))
                        for h in range(D // 512):
                            for i, (a, c) in enumerate(((0, 0), (0, 1), (1, 0))):
                                for k in range(KD):
                                    m = pe.matmul(acc[b][:, h * 512:(h + 1) * 512], mT[b][:, a, k, :],
                                                  w[:, c, k, h * 512:(h + 1) * 512], start=(i == 0 and k == 0),
                                                  stop=(i == 2 and k == KD - 1))
                        m.then_inc(mm.sem, 1)
                pairs(pe, body)


N_ROUTE = NG + NE
C_PICK4, C_PICK32, C_TILE, C_JOB = 0, 4, 36, 46
N_SMALL = C_JOB + MAX_JOBS


def stage_experts(nc, io, scr, l, nq, out):
    with Stage(nc, f"experts{l}") as st:
        logits = st.sb("logits", [P, nq, N_ROUTE])
        row_of = st.sb("row_of", [P, 2, nq], I32)
        weight = st.sb("weight", [P, 2, nq])
        jobs = st.sb("jobs", [1, MAX_JOBS], I32)
        more_pairs = st.sb("more_pairs", [1, 1], I32)
        ident = st.sb("ident", [P, P])
        with ExitStack() as inner:
            route_logits(nc, io, scr, l, nq, st, inner, ident, logits)
        with ExitStack() as inner:
            deal_rows(nc, io, scr, nq, st, inner, logits, row_of, weight, jobs, more_pairs)
        with ExitStack() as inner:
            run_experts(nc, io, scr, l, nq, st, inner, ident, jobs, more_pairs)
        with ExitStack() as inner:
            combine(nc, io, scr, l, nq, st, inner, row_of, weight, out)


def route_logits(nc, io, scr, l, nq, st, inner, ident, logits):
    shift = st.sb("shift_rows", [P, 2, D], F32, inner)
    scale = st.sb("scale_rows", [P, 2, D], F32, inner)
    wr = st.sb("w_router", [P, KD, N_ROUTE], F32, inner)
    x = [st.sb(f"x_tile{b}", [P, D], F32, inner) for b in range(2)]
    h = [st.sb(f"h_tile{b}", [P, D], F32, inner) for b in range(2)]
    hT = [st.sb(f"hT_tile{b}", [P, KD, P], F32, inner) for b in range(2)]
    square = st.sb("square", [P, D], F32, inner)
    stat = st.sb("norm_stat", [P, 2, 4], F32, inner)
    acc = [st.ps(f"hT_acc{b}", [P, D], inner) for b in range(2)]
    lg = [st.ps(f"logit_acc{b}", [P, 512], inner) for b in range(2)]
    const_in, rows_in = st.dma("ident_loaded"), st.dma("mod_rows_loaded")
    x_in = [st.dma(f"x_loaded{b}") for b in range(2)]
    h_out = [st.pool_dma(f"h2_stored{b}") for b in range(2)]
    sq, ms, rt, rs, plus1, sc, hd, tr, cp, mm, lc = (st.event(n) for n in (
        "squares", "mean_square", "root", "rstd", "scale_plus_1", "scaled", "h_ready", "h_transposed",
        "hT_copied", "logit_products", "logits_copied"))

    def pairs(eng, body):
        body(0, 0)
        with eng.Fori(1, NL // 2) as p:
            body(p, 0)
        if nq > NL:
            body(NL // 2, 1)

    with nc.Block() as block:
        @block.sync
        def _(sp):
            sp.dma_start(ident[:, :], io["k_ident"]).then_inc(const_in.sem, 16)
            sp.dma_start(wr[:, :, :], io["w_router"][l]).then_inc(const_in.sem, 16)
            mod_rows(scr, l, 3, shift[:, :, :], sp).then_inc(rows_in.sem, 16)
            mod_rows(scr, l, 4, scale[:, :, :], sp).then_inc(rows_in.sem, 16)

            def body(p, who):
                for b in range(2):
                    t = p * 2 + b
                    if later(t, 2):
                        sp.wait_ge(sc.sem, sc.done(t - 2))
                    sp.dma_start(x[b][:, :], scr["x1"][ds(t * P, P), :]).then_inc(x_in[b].sem, 16)
            pairs(sp, body)

        @block.gpsimd
        def _(pool):
            def body(p, who):
                for b in range(2):
                    t = p * 2 + b
                    pool.wait_ge(hd.sem, hd.done(t))
                    pool.dma_start(scr["h2"][ds(t * P, P), :], h[b][:, :]).then_inc(h_out[b].sem, 16)
            pairs(pool, body)
            for b in range(2):
                pool.wait_ge(h_out[b].sem, h_out[b].done(nq // 2 - 1))

        @block.scalar
        def _(act):
            def copy(t, b):
                act.wait_ge(tr.sem, tr.done(t))
                if later(t, 2):
                    act.wait_ge(mm.sem, mm.done(t - 2))
                act.copy(hT[b][:, :, :], acc[b][:, :].rearrange("p (k n) -> p k n", k=KD)).then_inc(cp.sem, 1)

            def body(p, who):
                for b in range(2):
                    t = p * 2 + b
                    act.wait_ge(x_in[b].sem, x_in[b].done(p))
                    act.activation(square[:, :], x[b][:, :], ACT.Square,
                                   accum_out=stat[:, b, 0:1]).then_inc(sq.sem, 1)
                    act.wait_ge(ms.sem, ms.done(t))
                    act.activation(stat[:, b, 2:3], stat[:, b, 1:2], ACT.Sqrt).then_inc(rt.sem, 1)
                    if not isinstance(t, int) or t > 0:
                        copy(t - 1, 1 - b)
            pairs(act, body)
            copy(nq - 1, 1)

        @block.vector
        def _(dve):
            dve.wait_ge(rows_in.sem, rows_in.done(1))
            dve.tensor_scalar(scale[:, :, :], scale[:, :, :], 1.0, None, ALU.add).then_inc(plus1.sem, 1)
            dve.wait_ge(plus1.sem, plus1.done(0))

            def take(t, b):
                dve.wait_ge(mm.sem, mm.done(t))
                dve.tensor_copy(logits[:, ds(t, 1), :].rearrange("p o n -> p (o n)"), lg[b][:, 0:N_ROUTE]
                                ).then_inc(lc.sem, 1)

            def body(p, who):
                for b in range(2):
                    t = p * 2 + b
                    dve.wait_ge(sq.sem, sq.done(t))
                    dve.tensor_scalar(stat[:, b, 1:2], stat[:, b, 0:1], 1.0 / D, EPS, ALU.mult, ALU.add
                                      ).then_inc(ms.sem, 1)
                    dve.wait_ge(rt.sem, rt.done(t))
                    dve.reciprocal(stat[:, b, 3:4], stat[:, b, 2:3]).then_inc(rs.sem, 1)
                    dve.wait_ge(rs.sem, rs.done(t))
                    if later(t, 2):
                        dve.wait_ge(tr.sem, tr.done(t - 2))
                    if later(p, 1):
                        dve.wait_ge(h_out[b].sem, h_out[b].done(p - 1))
                    dve.scalar_tensor_tensor(out=h[b][:, :], in0=x[b][:, :], scalar=stat[:, b, 3:4],
                                             in1=scale[:, who, :], op0=ALU.mult, op1=ALU.mult).then_inc(sc.sem, 1)
                    dve.wait_ge(sc.sem, sc.done(t))
                    dve.tensor_tensor(h[b][:, :], h[b][:, :], shift[:, who, :], ALU.add).then_inc(hd.sem, 1)
                    if later(t, 2):
                        take(t - 2, b)
            pairs(dve, body)
            take(nq - 2, 0)
            take(nq - 1, 1)

        @block.tensor
        def _(pe):
            pe.wait_ge(const_in.sem, const_in.done(1))

            def products(t, b):
                pe.wait_ge(cp.sem, cp.done(t))
                if later(t, 2):
                    pe.wait_ge(lc.sem, lc.done(t - 2))
                for k in range(KD):
                    m = pe.matmul(lg[b][:, 0:N_ROUTE], hT[b][:, k, :], wr[:, k, :], start=(k == 0), stop=(k == KD - 1))
                m.then_inc(mm.sem, 1)

            def body(p, who):
                for b in range(2):
                    t = p * 2 + b
                    if not isinstance(t, int) or t > 1:
                        pe.wait_ge(cp.sem, cp.done(t - 2))
                    pe.wait_ge(hd.sem, hd.done(t))
                    for k in range(KD):
                        m = pe.transpose(acc[b][:, k * P:(k + 1) * P], h[b][:, k * P:(k + 1) * P], ident[:, :])
                    m.then_inc(tr.sem, 1)
                    if not isinstance(t, int) or t > 0:
                        products(t - 1, 1 - b)
            pairs(pe, body)
            products(nq - 1, 1)


def deal_rows(nc, io, scr, nq, st, inner, logits, row_of, weight, jobs, more_pairs):
    def sb(name, shape, dt=F32):
        return st.sb(name, shape, dt, inner)

    small = sb("small", [P, N_SMALL])
    token = sb("token", [P, NT], I32)
    zeros = sb("zeros", [P, MAX_JOBS], I32)
    earlier = sb("earlier", [P, P])
    earlier_b, ones_b = sb("earlier_bf16", [P, P], BF16), sb("ones_bf16", [P, P], BF16)
    both_b = sb("both_bf16", [P, nq, NE], BF16)
    g_max, g_sum, g_w = sb("g_max", [P, nq]), sb("g_sum", [P, nq]), sb("g_w", [P, nq])
    g_rel, g_exp, g_hot = sb("g_rel", [P, nq, NG]), sb("g_exp", [P, nq, NG]), sb("g_hot", [P, nq, NG])
    g_soft = sb("g_soft", [P, nq, NG])
    e_in = [sb(f"e_in{c}", [P, nq, NE]) for c in range(2)]
    hot = [sb(f"hot{c}", [P, nq, NE]) for c in range(2)]
    top, pick = [sb(f"top{c}", [P, nq]) for c in range(2)], sb("pick", [P, nq])
    both, place, placed = sb("both", [P, nq, NE]), sb("place", [P, nq, NE]), sb("placed", [P, nq, NE])
    rel, rel_exp, denom = sb("rel", [P, nq]), sb("rel_exp", [P, nq]), sb("denom", [P, nq])
    rows_f = sb("rows_f", [P, 2, nq])
    more = sb("more", [P, NE, NT])
    tiles, tiles_sum, base, one_row = sb("tiles", [P, NE]), sb("tiles_sum", [P, NE]), sb("base", [P, NE]), sb("one_row", [P, NE])
    ended = sb("ended", [1, MAX_JOBS, NE])
    job_f, pairs_f = sb("job_f", [1, MAX_JOBS]), sb("pairs_f", [1, 2])
    acc = st.ps("rank_acc", [P, nq + 1, NE], inner)
    ld, zeroed, filled = st.dma("small_loaded"), st.event("zeros_ready"), st.pool_dma("token_of_cleared")
    scat = st.pool_dma("token_of_filled")
    dv, ex, mm = st.event("routing_step"), st.event("routing_exp"), st.event("ranks_done")
    J = MAX_JOBS

    with nc.Block() as block:
        @block.sync
        def _(sp):
            sp.dma_start(small[:, :], io["k_small"]).then_inc(ld.sem, 16)
            sp.dma_start(token[:, :], io["k_token"]).then_inc(ld.sem, 16)
            sp.dma_start(earlier[:, :], io["k_earlier"]).then_inc(ld.sem, 16)

        n_dve, marks = [0], {}

        @block.vector
        def _(dve):
            def step(ins):
                ins.then_inc(dv.sem, 1)
                n_dve[0] += 1
                dve.wait_ge(dv.sem, dv.done(n_dve[0] - 1))

            def wide(ap, n):
                return ap.unsqueeze(2).to_broadcast([P, nq, n])

            def const(c, n):
                return small[:, c:c + n].unsqueeze(1).to_broadcast([P, nq, n])

            def first_of(values, best, n, col, scratch, dst):
                step(dve.tensor_tensor(scratch, values, wide(best, n), ALU.is_equal))
                step(dve.tensor_tensor(scratch, scratch, const(col, n), ALU.mult))
                step(dve.tensor_reduce(pick[:, :], scratch, AX.X, ALU.max))
                step(dve.tensor_tensor(dst, scratch, wide(pick[:, :], n), ALU.is_equal))

            dve.wait_ge(ld.sem, ld.done(2))
            step(dve.memset(ones_b[:, :], 1.0))
            step(dve.tensor_copy(earlier_b[:, :], earlier[:, :]))
            step(dve.memset(one_row[:, :], 1.0))
            g = logits[:, :, 0:NG]
            step(dve.tensor_reduce(g_max[:, :], g, AX.X, ALU.max))
            step(dve.tensor_tensor(g_rel[:, :, :], g, wide(g_max[:, :], NG), ALU.subtract))
            first_of(g, g_max[:, :], NG, C_PICK4, g_exp[:, :, :], g_hot[:, :, :])
            step(dve.tensor_scalar(g_exp[:, :, :], g_hot[:, :, :], 1.0, 1e30, ALU.subtract, ALU.mult))
            step(dve.tensor_tensor(e_in[0][:, :, :].rearrange("p t (g e) -> p t g e", g=NG),
                                   logits[:, :, NG:].rearrange("p t (g e) -> p t g e", g=NG),
                                   g_exp[:, :, :].unsqueeze(3).to_broadcast([P, nq, NG, EG]), ALU.add))
            for c in range(2):
                step(dve.tensor_reduce(top[c][:, :], e_in[c][:, :, :], AX.X, ALU.max))
                first_of(e_in[c][:, :, :], top[c][:, :], NE, C_PICK32, both[:, :, :], hot[c][:, :, :])
                if c == 0:
                    step(dve.scalar_tensor_tensor(out=e_in[1][:, :, :], in0=hot[0][:, :, :], scalar=-3e30,
                                                  in1=e_in[0][:, :, :], op0=ALU.mult, op1=ALU.add))
            step(dve.tensor_tensor(both_b[:, :, :], hot[0][:, :, :], hot[1][:, :, :], ALU.add))
            marks["both"] = n_dve[0]
            step(dve.tensor_tensor(rel[:, :], top[1][:, :], top[0][:, :], ALU.subtract))
            marks["rel"] = n_dve[0]
            dve.wait_ge(ex.sem, ex.done(1))
            step(dve.tensor_reduce(g_sum[:, :], g_soft[:, :, :], AX.X, ALU.add))
            step(dve.reciprocal(g_w[:, :], g_sum[:, :]))
            step(dve.tensor_scalar(denom[:, :], rel_exp[:, :], 1.0, None, ALU.add))
            step(dve.reciprocal(rel[:, :], denom[:, :]))
            step(dve.tensor_tensor(weight[:, 0, :], rel[:, :], g_w[:, :], ALU.mult))
            step(dve.tensor_tensor(weight[:, 1, :], weight[:, 0, :], rel_exp[:, :], ALU.mult))
            dve.wait_ge(mm.sem, mm.done(0))
            step(dve.tensor_copy(base[:, :], acc[:, nq, :]))
            step(dve.tensor_tensor(more[:, :, :], base[:, :].unsqueeze(2).to_broadcast([P, NE, NT]),
                                   small[:, C_TILE:C_TILE + NT].unsqueeze(1).to_broadcast([P, NE, NT]), ALU.is_gt))
            step(dve.tensor_reduce(tiles[:, :], more[:, :, :], AX.X, ALU.add))
            step(dve.tensor_tensor_scan(tiles_sum[:, :], one_row[:, :], tiles[:, :], 0.0, ALU.mult, ALU.add))
            step(dve.tensor_tensor(base[:, :], tiles_sum[:, :], tiles[:, :], ALU.subtract))
            step(dve.tensor_scalar(base[:, :], base[:, :], float(P), None, ALU.mult))
            step(dve.tensor_tensor(place[:, :, :], acc[:, 0:nq, :],
                                   base[:, :].unsqueeze(1).to_broadcast([P, nq, NE]), ALU.add))
            for c in range(2):
                step(dve.tensor_tensor(placed[:, :, :], place[:, :, :], hot[c][:, :, :], ALU.mult))
                step(dve.tensor_reduce(rows_f[:, c, :], placed[:, :, :], AX.X, ALU.add))
            step(dve.tensor_copy(row_of[:, :, :], rows_f[:, :, :]))
            marks["rows"] = n_dve[0]
            step(dve.tensor_tensor(ended[:, :, :], tiles_sum[0:1, :].unsqueeze(1).to_broadcast([1, J, NE]),
                                   small[0:1, C_JOB:C_JOB + J].unsqueeze(2).to_broadcast([1, J, NE]), ALU.is_le))
            step(dve.tensor_reduce(job_f[:, :], ended[:, :, :], AX.X, ALU.add))
            step(dve.tensor_scalar(jobs[:, :], job_f[:, :], float(NE - 1), None, ALU.min))
            step(dve.tensor_scalar(ended[:, 0:J // 2, 0], small[0:1, C_JOB:C_JOB + J:2],
                                   tiles_sum[0:1, NE - 1:NE], None, ALU.is_lt))
            step(dve.tensor_reduce(pairs_f[:, 0:1], ended[:, 0:J // 2, 0], AX.X, ALU.add))
            step(dve.tensor_scalar(more_pairs[:, :], pairs_f[:, 0:1], float(nq), None, ALU.subtract))

        @block.scalar
        def _(act):
            act.wait_ge(dv.sem, dv.done(marks["rel"] - 1))
            act.activation(g_soft[:, :, :], g_rel[:, :, :], ACT.Exp).then_inc(ex.sem, 1)
            act.activation(rel_exp[:, :], rel[:, :], ACT.Exp).then_inc(ex.sem, 1)

        @block.tensor
        def _(pe):
            pe.wait_ge(dv.sem, dv.done(marks["both"] - 1))
            for t in range(nq + 1):
                for u in range(min(t, nq - 1) + 1):
                    m = pe.matmul(acc[:, t, :], (earlier_b if u == t else ones_b)[:, :], both_b[:, u, :],
                                  start=(u == 0), stop=(u == min(t, nq - 1)))
            m.then_inc(mm.sem, 1)

        @block.gpsimd
        def _(pool):
            pool.memset(zeros[:, :], 0).then_inc(zeroed.sem, 1)
            pool.wait_ge(zeroed.sem, zeroed.done(0))
            pool.dma_start(scr["token_of"].rearrange("(p j) o -> p (j o)", p=P), zeros[:, :]).then_inc(filled.sem, 16)
            pool.wait_ge(filled.sem, filled.done(0))
            pool.wait_ge(ld.sem, ld.done(2))
            pool.wait_ge(dv.sem, dv.done(marks["rows"] - 1))
            for c in range(2):
                for t in range(nq):
                    pool.indirect_dma_start(
                        out=scr["token_of"], out_offset=bass.IndirectOffsetOnAxis(
                            ap=row_of[:, c, t:t + 1].bitcast(U32), axis=0),
                        in_=token[:, t:t + 1], in_offset=None).then_inc(scat.sem, 16)
            pool.wait_ge(scat.sem, scat.done(2 * nq - 1))


def run_experts(nc, io, scr, l, nq, st, inner, ident, jobs, more_pairs):
    def sb(name, shape, dt=F32):
        return st.sb(name, shape, dt, inner)

    HK = EH // P
    lo, hi = nq, MAX_JOBS // 2
    w_gate = [sb(f"w_gate{b}", [P, KD, EH]) for b in range(2)]
    w_up = [sb(f"w_up{b}", [P, KD, EH]) for b in range(2)]
    w_down = [sb(f"w_down{b}", [P, HK, D]) for b in range(2)]
    index = [sb(f"index{b}", [P, 1], I32) for b in range(2)]
    x = [sb(f"rows{b}", [P, D]) for b in range(2)]
    xT = sb("rowsT", [P, KD, P])
    act_g = sb("silu_gate", [P, EH])
    hidden = sb("hidden", [P, EH])
    hT = [sb(f"hiddenT{b}", [P, HK, P]) for b in range(2)]
    y = [sb(f"result{b}", [P, D]) for b in range(2)]
    acc_x = st.ps("rowsT_acc", [P, D], inner)
    acc_g, acc_u = st.ps("gate_acc", [P, EH], inner), st.ps("up_acc", [P, EH], inner)
    acc_h = st.ps("hiddenT_acc", [P, EH], inner)
    acc_y = st.ps("result_acc", [P, D], inner)
    i_in, x_in = ([st.pool_dma(f"{n}{b}") for b in range(2)] for n in ("index_loaded", "rows_gathered"))
    gu_in, d_in, y_out = ([st.dma(f"{n}{b}") for b in range(2)] for n in (
        "w_gate_up_loaded", "w_down_loaded", "result_stored"))
    taken, ended = st.event("pool_waits_taken"), st.event("result_waits_taken")
    xt, xa, xd, gm, um, sg, hm, ht, hc, dm, ya, yd = (st.event(n) for n in (
        "rows_transposed", "rowsT_by_act", "rowsT_by_dve", "gate_products", "up_products", "silu_done",
        "hidden_ready", "hidden_transposed", "hiddenT_copied", "down_products", "result_by_act", "result_by_dve"))

    def load_count(eng):
        return eng.value_load(more_pairs[0:1, 0:1], min_val=0, max_val=hi - lo) + lo

    def pairs(eng, n, body):
        body(0, False)
        with eng.Fori(1, n - 1) as i:
            body(i, False)
        body(n - 1, True)

    with nc.Block() as block:
        @block.sync
        def _(sp):
            n = load_count(sp)

            def body(i, last):
                for b in range(2):
                    g = i * 2 + b
                    e = sp.value_load(jobs[0:1, ds(g, 1)], min_val=0, max_val=NE - 1)
                    if later(g, 2):
                        sp.wait_ge(um.sem, um.done(g - 2))
                    for w, name in ((w_gate, "w_exp_gate"), (w_up, "w_exp_up")):
                        sp.dma_start(w[b][:, :, :], io[name][l, ds(e, 1), :, :].rearrange(
                            "o (k p) n -> p (o k) n", p=P)).then_inc(gu_in[b].sem, 16)
                    if later(g, 2):
                        sp.wait_ge(dm.sem, dm.done(g - 2))
                    sp.dma_start(w_down[b][:, :, :], io["w_exp_down"][l, ds(e, 1), :, :].rearrange(
                        "o (k p) n -> p (o k) n", p=P)).then_inc(d_in[b].sem, 16)
            pairs(sp, n, body)

        @block.gpsimd
        def _(pool):
            n = load_count(pool)

            def body(i, last):
                for b in range(2):
                    g = i * 2 + b
                    if later(i, 1):
                        pool.wait_ge(x_in[b].sem, x_in[b].done(i - 1))
                    pool.dma_start(index[b][:, :], scr["token_of"][ds(g * P, P), :]).then_inc(i_in[b].sem, 16)
                    pool.wait_ge(i_in[b].sem, i_in[b].done(i))
                    if later(g, 2):
                        pool.wait_ge(xt.sem, xt.done(g - 2))
                    take_waits(pool, taken)
                    pool.indirect_dma_start(
                        out=x[b][:, :], out_offset=None, in_=scr["h2"],
                        in_offset=bass.IndirectOffsetOnAxis(ap=index[b][:, :].bitcast(U32), axis=0)
                    ).then_inc(x_in[b].sem, 16)
            pairs(pool, n, body)

        @block.scalar
        def _(act):
            n = load_count(act)

            def copy_rows(g):
                act.wait_ge(xt.sem, xt.done(g))
                act.copy(xT[:, 0:KD // 2, :], acc_x[:, 0:D // 2].rearrange("p (k n) -> p k n", n=P)).then_inc(xa.sem, 1)

            def result(g, b, i):
                act.wait_ge(dm.sem, dm.done(g))
                if later(i, 1):
                    act.wait_ge(y_out[b].sem, y_out[b].done(i - 1))
                act.copy(y[b][:, 0:D // 2], acc_y[:, 0:D // 2]).then_inc(ya.sem, 1)
                act.wait_ge(ya.sem, ya.done(g))
                act.wait_ge(yd.sem, yd.done(g))
                act.dma_start(scr["ye"][ds(g * P, P), :], y[b][:, :]).then_inc(y_out[b].sem, 16)

            def body(i, last):
                for b in range(2):
                    g = i * 2 + b
                    act.wait_ge(gm.sem, gm.done(g))
                    if later(g, 1):
                        act.wait_ge(hm.sem, hm.done(g - 1))
                    act.activation(act_g[:, :], acc_g[:, :], ACT.Silu).then_inc(sg.sem, 1)
                    if not (last and b):
                        copy_rows(g + 1)
                    if not isinstance(g, int) or g > 0:
                        result(g - 1, 1 - b, i if b else i - 1)
            copy_rows(0)
            pairs(act, n, body)
            result(n * 2 - 1, 1, n - 1)
            for b in range(2):
                act.wait_ge(y_out[b].sem, y_out[b].done(n - 1))
            take_waits(act, ended)

        @block.vector
        def _(dve):
            n = load_count(dve)

            def copy_rows(g):
                dve.wait_ge(xt.sem, xt.done(g))
                dve.tensor_copy(xT[:, KD // 2:, :], acc_x[:, D // 2:].rearrange("p (k n) -> p k n", n=P)
                                ).then_inc(xd.sem, 1)

            def result(g, b, i):
                dve.wait_ge(dm.sem, dm.done(g))
                if later(i, 1):
                    dve.wait_ge(y_out[b].sem, y_out[b].done(i - 1))
                dve.tensor_copy(y[b][:, D // 2:], acc_y[:, D // 2:]).then_inc(yd.sem, 1)

            def body(i, last):
                for b in range(2):
                    g = i * 2 + b
                    dve.wait_ge(sg.sem, sg.done(g))
                    dve.wait_ge(um.sem, um.done(g))
                    if later(g, 1):
                        dve.wait_ge(ht.sem, ht.done(g - 1))
                    dve.tensor_tensor(hidden[:, :], act_g[:, :], acc_u[:, :], ALU.mult).then_inc(hm.sem, 1)
                    if not (last and b):
                        copy_rows(g + 1)
                    if not isinstance(g, int) or g > 0:
                        result(g - 1, 1 - b, i if b else i - 1)
                    dve.wait_ge(ht.sem, ht.done(g))
                    if later(g, 2):
                        dve.wait_ge(dm.sem, dm.done(g - 2))
                    dve.tensor_copy(hT[b][:, :, :], acc_h[:, :].rearrange("p (k n) -> p k n", n=P)).then_inc(hc.sem, 1)
            copy_rows(0)
            pairs(dve, n, body)
            result(n * 2 - 1, 1, n - 1)

        @block.tensor
        def _(pe):
            n = load_count(pe)

            def transpose_rows(g, b, i):
                pe.wait_ge(x_in[b].sem, x_in[b].done(i))
                if later(g, 1):
                    pe.wait_ge(xa.sem, xa.done(g - 1))
                if later(g, 1):
                    pe.wait_ge(xd.sem, xd.done(g - 1))
                for k in range(KD):
                    m = pe.transpose(acc_x[:, k * P:(k + 1) * P], x[b][:, k * P:(k + 1) * P], ident[:, :])
                m.then_inc(xt.sem, 1)

            def down(g, b, i):
                pe.wait_ge(hc.sem, hc.done(g))
                pe.wait_ge(d_in[b].sem, d_in[b].done(i))
                if later(g, 1):
                    pe.wait_ge(ya.sem, ya.done(g - 1))
                if later(g, 1):
                    pe.wait_ge(yd.sem, yd.done(g - 1))
                for h in range(D // 512):
                    for k in range(HK):
                        m = pe.matmul(acc_y[:, h * 512:(h + 1) * 512], hT[b][:, k, :],
                                      w_down[b][:, k, h * 512:(h + 1) * 512], start=(k == 0), stop=(k == HK - 1))
                m.then_inc(dm.sem, 1)

            def body(i, last):
                for b in range(2):
                    g = i * 2 + b
                    pe.wait_ge(xa.sem, xa.done(g))
                    pe.wait_ge(xd.sem, xd.done(g))
                    pe.wait_ge(gu_in[b].sem, gu_in[b].done(i * 2 + 1))
                    if later(g, 1):
                        pe.wait_ge(sg.sem, sg.done(g - 1))
                    for k in range(KD):
                        m = pe.matmul(acc_g[:, :], xT[:, k, :], w_gate[b][:, k, :], start=(k == 0), stop=(k == KD - 1))
                    m.then_inc(gm.sem, 1)
                    if later(g, 1):
                        pe.wait_ge(hm.sem, hm.done(g - 1))
                    for k in range(KD):
                        m = pe.matmul(acc_u[:, :], xT[:, k, :], w_up[b][:, k, :], start=(k == 0), stop=(k == KD - 1))
                    m.then_inc(um.sem, 1)
                    if not (last and b):
                        transpose_rows(g + 1, 1 - b, i + b)
                    if not isinstance(g, int) or g > 0:
                        down(g - 1, 1 - b, i if b else i - 1)
                    pe.wait_ge(hm.sem, hm.done(g))
                    if later(g, 1):
                        pe.wait_ge(hc.sem, hc.done(g - 1))
                    for k in range(HK):
                        m = pe.transpose(acc_h[:, k * P:(k + 1) * P], hidden[:, k * P:(k + 1) * P], ident[:, :])
                    m.then_inc(ht.sem, 1)
            transpose_rows(0, 0, 0)
            pairs(pe, n, body)
            down(n * 2 - 1, 1, n - 1)


def combine(nc, io, scr, l, nq, st, inner, row_of, weight, out):
    SLOTS = 4
    gate = st.sb("gate_rows", [P, 2, D], F32, inner)
    x = [st.sb(f"x{b}", [P, D], F32, inner) for b in range(SLOTS)]
    y = [[st.sb(f"y{c}_{b}", [P, D], F32, inner) for b in range(SLOTS)] for c in range(2)]
    rows_in = st.dma("gate_loaded")
    x_in = [st.dma(f"x1_loaded{b}") for b in range(SLOTS)]
    y_in = [[st.pool_dma(f"y{c}_gathered{b}") for b in range(SLOTS)] for c in range(2)]
    stored = [st.dma(f"x2_stored{b}") for b in range(SLOTS)]
    m1, m2, m3, m4 = (st.event(n) for n in ("first_weighted", "second_added", "gated", "x2_ready"))

    with nc.Block() as block:
        @block.sync
        def _(sp):
            mod_rows(scr, l, 5, gate[:, :, :], sp).then_inc(rows_in.sem, 16)
            for t in range(nq):
                b = t % SLOTS
                if later(t, SLOTS):
                    sp.wait_ge(m4.sem, m4.done(t - SLOTS))
                sp.dma_start(x[b][:, :], scr["x1"][t * P:(t + 1) * P, :]).then_inc(x_in[b].sem, 16)

        @block.gpsimd
        def _(pool):
            for t in range(nq):
                b = t % SLOTS
                if later(t, SLOTS):
                    pool.wait_ge(m2.sem, m2.done(t - SLOTS))
                if later(t, SLOTS):
                    pool.wait_ge(stored[b].sem, stored[b].done(t // SLOTS - 1))
                for c in range(2):
                    pool.indirect_dma_start(
                        out=y[c][b][:, :], out_offset=None, in_=scr["ye"],
                        in_offset=bass.IndirectOffsetOnAxis(ap=row_of[:, c, t:t + 1].bitcast(U32), axis=0)
                    ).then_inc(y_in[c][b].sem, 16)

        @block.vector
        def _(dve):
            dve.wait_ge(rows_in.sem, rows_in.done(0))
            for t in range(nq):
                b, who = t % SLOTS, t // NL
                dve.wait_ge(y_in[0][b].sem, y_in[0][b].done(t // SLOTS))
                dve.wait_ge(y_in[1][b].sem, y_in[1][b].done(t // SLOTS))
                dve.tensor_scalar(y[0][b][:, :], y[0][b][:, :], weight[:, 0, t:t + 1], None, ALU.mult
                                  ).then_inc(m1.sem, 1)
                dve.wait_ge(m1.sem, m1.done(t))
                dve.scalar_tensor_tensor(out=y[0][b][:, :], in0=y[1][b][:, :], scalar=weight[:, 1, t:t + 1],
                                         in1=y[0][b][:, :], op0=ALU.mult, op1=ALU.add).then_inc(m2.sem, 1)
                dve.wait_ge(m2.sem, m2.done(t))
                dve.tensor_tensor(y[0][b][:, :], y[0][b][:, :], gate[:, who, :], ALU.mult).then_inc(m3.sem, 1)
                dve.wait_ge(m3.sem, m3.done(t))
                dve.wait_ge(x_in[b].sem, x_in[b].done(t // SLOTS))
                dve.tensor_tensor(y[0][b][:, :], y[0][b][:, :], x[b][:, :], ALU.add).then_inc(m4.sem, 1)

        @block.scalar
        def _(act):
            for t in range(nq):
                b = t % SLOTS
                act.wait_ge(m4.sem, m4.done(t))
                dst = out[0, t * P:(t + 1) * P, :] if l == DEPTH - 1 else scr["x2"][t * P:(t + 1) * P, :]
                act.dma_start(dst, y[0][b][:, :]).then_inc(stored[b].sem, 16)
            for b in range(SLOTS):
                act.wait_ge(stored[b].sem, stored[b].done((nq - 1 - b) // SLOTS))


def host_constants():
    rows = SEQ // GRID_W
    row = np.repeat(np.arange(rows, dtype=np.float32), GRID_W)
    col = np.tile(np.arange(GRID_W, dtype=np.float32), rows)
    freqs = np.float32(THETA) ** (-np.arange(HD // 4, dtype=np.float32) / np.float32(HD // 4))
    ang = np.concatenate([row[:, None] * freqs, col[:, None] * freqs], axis=-1).astype(np.float32)
    cos, sin = np.cos(ang), np.sin(ang)
    rope = np.zeros((NL + 1, P, 2, HD), np.float32)
    rope[:NL, :, 0] = np.concatenate([cos, cos], -1).reshape(NL, P, HD)
    rope[:NL, :, 1] = np.concatenate([-sin, sin], -1).reshape(NL, P, HD)
    rope[NL, :, 0] = 1.0
    i = np.arange(P)
    band = np.zeros((P, 3, P), np.float32)
    band[:, 0][i[None, :] < i[:, None]] = NEG
    band[:, 2][i[None, :] > i[:, None]] = NEG
    small = np.concatenate([np.arange(NG, 0, -1), np.arange(NE, 0, -1), P * np.arange(NT), np.arange(MAX_JOBS)])
    return {"k_small": np.tile(small.astype(np.float32), (P, 1)),
            "k_token": (np.arange(NT)[None, :] * P + i[:, None]).astype(np.int32),
            "k_rope": rope, "k_band": band, "k_ident": np.eye(P, dtype=np.float32),
            "k_earlier": (i[:, None] < i[None, :]).astype(np.float32)}


def laid_out(inputs):
    cols = [np.asarray(inputs["c"]).reshape(KD, P).T, np.asarray(inputs["c_ctx"]).reshape(KD, P).T]
    w = np.asarray(inputs["w_in"])
    order = [w[:, :, a:a + n] for a, n in ((A_Q, 512), (B_Q, 512), (C_Q, 512), (B_K, 512), (A_K, P), (C_K, P),
                                           (A_V, P), (C_V, P), (B_V, 512))]
    gates = w[:, :, GATES:A_K].reshape(DEPTH, KD, P, 3, KD, P).transpose(0, 4, 3, 2, 1, 5)
    branches = np.stack([np.asarray(inputs[f"w_branch_{b}"]) for b in "abc"], 1)
    branches = branches.reshape(DEPTH, 3, 4, P, KD, P).transpose(0, 4, 1, 3, 2, 5)
    router = np.concatenate([np.asarray(inputs["w_router_group"]), np.asarray(inputs["w_router_expert"])], -1)
    return {"w_router": np.ascontiguousarray(router.reshape(DEPTH, KD, P, NG + NE).transpose(0, 2, 1, 3)),
            "c_cols": np.ascontiguousarray(np.stack(cols, axis=-1)),
            "w_heads": np.concatenate(order, axis=-1),
            "w_merge": np.ascontiguousarray(np.concatenate([gates, branches], axis=4))}


def build(nc, io, out, upto=99):
    scr = {n: nc.dram_tensor(n, list(s), dt).ap() for n, s, dt in (
        ("mod", (DEPTH, 2, N_MOD * D), F32),
        ("hT", (2, P, KD, T), F32),
        ("qk", (QK_SLOTS, P, T), F32),
        ("v", (T, V_COLS), F32),
        ("y", (T, Y_COLS), F32),
        ("mT", (2, P, KD, T), F32),
        ("x1", (T, D), F32), ("x2", (T, D), F32),
        ("h2", (T, D), F32),
        ("token_of", (MAX_JOBS * P, 1), I32),
        ("ye", (MAX_JOBS * P, D), F32),
    )}
    plan = [lambda: stage_modulation(nc, io, scr)]
    for l in range(DEPTH):
        nq = NT if l < DEPTH - 1 else NL
        plan += [
            lambda l=l, nq=nq: stage_project(nc, io, scr, l, nq),
            lambda l=l, nq=nq: stage_attend_a(nc, io, scr, l, nq),
            lambda l=l, nq=nq: stage_attend_b(nc, io, scr, l, nq),
            lambda l=l, nq=nq: stage_attend_c(nc, io, scr, l, nq),
            lambda l=l, nq=nq: stage_merge(nc, io, scr, l, nq),
            lambda l=l, nq=nq: stage_output(nc, io, scr, l, nq),
            lambda l=l, nq=nq: stage_experts(nc, io, scr, l, nq, out),
        ]
    with ExitStack() as Stage.whole_kernel:
        for stage in plan[:upto]:
            stage()


_INS = ["x", "ctx", "w_ada", "b_ada", "a_qnorm", "a_knorm", "b_qnorm", "b_knorm", "c_qnorm", "c_knorm",
        "lambda_q1", "lambda_k1", "lambda_q2", "lambda_k2", "b_subln", "c_sink", "w_out",
        "w_exp_gate", "w_exp_up", "w_exp_down"]


def kernel(**inputs):
    import concourse.bacc as _bacc
    from concourse.bass_utils import run_bass_kernel_spmd as _run

    nc = _bacc.Bacc("TRN2", target_bir_lowering=False, num_devices=1)
    given = {n: inputs[n] for n in _INS}
    given.update(laid_out(inputs))
    given.update(host_constants())
    arrays, io = {}, {}
    for name, a in given.items():
        a = np.ascontiguousarray(a)
        arrays[f"in_{name}_dram"] = a
        io[name] = nc.dram_tensor(f"in_{name}_dram", a.shape, mybir.dt.from_np(a.dtype), kind="ExternalInput").ap()
    out = nc.dram_tensor("out_0_dram", (1, SEQ, D), F32, kind="ExternalOutput").ap()
    build(nc, io, out)
    r = _run(nc, [arrays], core_ids=[0])
    return r.results[0]["out_0_dram"]
```
